# Optimizing a Trainium2 kernel written in Bass

```python
import jax, jax.numpy as jnp
from jax import lax
import numpy as np

D_MODEL = 1024
BATCH = 1
SEQ = 1024
DEPTH = 1
DEC_BATCH = 8
DEC_SEQ = 8
PAST_LEN = 8192
PAGE_SIZE = 128

MIX_WIDTH = D_MODEL
WIDTH_A = MIX_WIDTH // 2
WIDTH_B = MIX_WIDTH - WIDTH_A
CHUNK = 128
HEADS_A = 8
HEAD_DIM_A = WIDTH_A // HEADS_A
POOL_WINDOWS = (2, 4, 8, 16)
POOL_GROUPS = len(POOL_WINDOWS)
POOL_GROUP_DIM = WIDTH_B // POOL_GROUPS
POOL_HIST = max(POOL_WINDOWS) - 1
PROJ_WIDTH = 2 * WIDTH_A + WIDTH_B
N_MEM = 256
X_HEADS = 4
X_HEAD_DIM = D_MODEL // X_HEADS
N_EXPERT_GROUPS = 4
EXPERTS_PER_GROUP = 4
N_EXPERTS = N_EXPERT_GROUPS * EXPERTS_PER_GROUP
TOP_K_INNER = 2
D_EXPERT = D_MODEL // 4
EPS = 1e-6

kernel_name = "hymba_gmlp_pool_hmoe_step"

def rmsnorm(x, g):
    xf = x.astype(jnp.float32)
    r = lax.rsqrt(jnp.mean(xf * xf, axis=-1, keepdims=True) + EPS)
    return (xf * r * g.astype(jnp.float32)).astype(x.dtype)

def chunk_spatial_gate(u, v, w_s, b_s):
    b, l, h, dh = v.shape
    n_chunks = -(-l // CHUNK)
    pad = n_chunks * CHUNK - l
    vp = jnp.pad(v, ((0, 0), (0, pad), (0, 0), (0, 0))).reshape(b, n_chunks, CHUNK, h, dh)
    causal = jnp.tril(jnp.ones((CHUNK, CHUNK), dtype=bool))
    ws = jnp.where(causal[None], w_s, jnp.zeros((), w_s.dtype))
    mixed = jnp.einsum('hij,bcjhd->bcihd', ws, vp) + b_s.T[None, None, :, :, None]
    mixed = mixed.reshape(b, n_chunks * CHUNK, h, dh)[:, :l]
    return u * mixed

def multiscale_pool(z_ext, pos0, w_pool, s_pool):
    b, le, _ = z_ext.shape
    l = le - POOL_HIST
    zf = z_ext.astype(jnp.float32)
    cs = jnp.concatenate([jnp.zeros((b, 1, WIDTH_B), jnp.float32), jnp.cumsum(zf, axis=1)], axis=1)
    end = cs[:, POOL_HIST + 1:]
    z_new = zf[:, POOL_HIST:]
    pos = pos0 + jnp.arange(l)
    outs = []
    for g, w in enumerate(POOL_WINDOWS):
        sl = slice(g * POOL_GROUP_DIM, (g + 1) * POOL_GROUP_DIM)
        start = cs[:, POOL_HIST + 1 - w:POOL_HIST + 1 - w + l, sl]
        cnt = jnp.minimum(w, pos + 1).astype(jnp.float32)[None, :, None]
        outs.append((end[..., sl] - start) / cnt - z_new[..., sl])
    pooled = jnp.stack(outs, axis=2).astype(z_ext.dtype)
    y = jnp.einsum('blgc,gcd->blgd', pooled, w_pool).reshape(b, l, WIDTH_B)
    return y * s_pool

def memory_attention(h, mem_k, mem_v, w_q, w_o):
    b, l, _ = h.shape
    q = (h @ w_q).reshape(b, l, X_HEADS, X_HEAD_DIM)
    s = jnp.einsum('blhd,bmhd->bhlm', q, mem_k).astype(jnp.float32) * (X_HEAD_DIM ** -0.5)
    p = jax.nn.softmax(s, axis=-1).astype(h.dtype)
    o = jnp.einsum('bhlm,bmhd->blhd', p, mem_v).reshape(b, l, D_MODEL)
    return o @ w_o

def hierarchical_moe(h, w_group, b_group, w_router, b_router, w_gate, w_up, w_down):
    b, l, d = h.shape
    t = h.reshape(b * l, d)
    g_logits = (t @ w_group).astype(jnp.float32) + b_group.astype(jnp.float32)
    g_prob = jax.nn.softmax(g_logits, axis=-1)
    g_idx = jnp.argmax(g_logits, axis=-1)
    g_p = jnp.max(g_prob, axis=-1, keepdims=True)
    e_logits = ((t @ w_router).astype(jnp.float32) + b_router.astype(jnp.float32)).reshape(
        -1, N_EXPERT_GROUPS, EXPERTS_PER_GROUP)
    e_sel = jnp.einsum('tge,tg->te', e_logits, jax.nn.one_hot(g_idx, N_EXPERT_GROUPS, dtype=jnp.float32))
    top_v, top_i = lax.top_k(e_sel, TOP_K_INNER)
    top_w = jax.nn.softmax(top_v, axis=-1) * g_p
    expert_id = g_idx[:, None] * EXPERTS_PER_GROUP + top_i
    gates = jnp.sum(jax.nn.one_hot(expert_id, N_EXPERTS, dtype=jnp.float32) * top_w[..., None], axis=1)
    hg = jnp.einsum('td,edf->tef', t, w_gate)
    hu = jnp.einsum('td,edf->tef', t, w_up)
    a = jax.nn.silu(hg) * hu * gates[..., None].astype(t.dtype)
    y = jnp.einsum('tef,efd->td', a, w_down)
    return y.reshape(b, l, d)

def layer_fwd(x, pos0, pool_hist, mem_k, mem_v,
              g_mix, w_in, g_v, w_s, b_s, w_pool, s_pool, w_out,
              g_xattn, w_xq, w_xo,
              g_ffn, w_group, b_group, w_router, b_router, w_gate, w_up, w_down):
    b, l, _ = x.shape
    h = rmsnorm(x, g_mix)
    proj = h @ w_in
    ua = jax.nn.gelu(proj[..., :2 * WIDTH_A])
    u = ua[..., :WIDTH_A].reshape(b, l, HEADS_A, HEAD_DIM_A)
    v = rmsnorm(ua[..., WIDTH_A:], g_v).reshape(b, l, HEADS_A, HEAD_DIM_A)
    z = proj[..., 2 * WIDTH_A:]
    a_out = chunk_spatial_gate(u, v, w_s, b_s).reshape(b, l, WIDTH_A)
    z_ext = jnp.concatenate([pool_hist.astype(z.dtype), z], axis=1)
    b_out = multiscale_pool(z_ext, pos0, w_pool, s_pool)
    x = x + jnp.concatenate([a_out, b_out], axis=-1) @ w_out
    x = x + memory_attention(rmsnorm(x, g_xattn), mem_k, mem_v, w_xq, w_xo)
    x = x + hierarchical_moe(rmsnorm(x, g_ffn), w_group, b_group, w_router, b_router, w_gate, w_up, w_down)
    last_chunk_start = ((l - 1) // CHUNK) * CHUNK
    return x, v[:, last_chunk_start:], z_ext[:, -POOL_HIST:]

def setup_inputs(seed: int = 0) -> dict:
    key = jax.random.key(seed)
    ks = jax.random.split(key, 32)
    f32 = jnp.float32

    def nrm(k, shape, s):
        return jax.random.normal(k, shape, f32) * s

    def gain(k, shape):
        return 1.0 + 0.02 * jax.random.normal(k, shape, f32)

    return {
        "x_prompt": nrm(ks[0], (BATCH, SEQ, D_MODEL), 1.0),
        "x_sample": nrm(ks[1], (DEC_BATCH, DEC_SEQ, D_MODEL), 1.0),
        "cache_mem_k": nrm(ks[2], (DEPTH, DEC_BATCH, N_MEM, X_HEADS, X_HEAD_DIM), 1.0),
        "cache_mem_v": nrm(ks[3], (DEPTH, DEC_BATCH, N_MEM, X_HEADS, X_HEAD_DIM), 1.0),
        "state_pool": nrm(ks[4], (DEPTH, DEC_BATCH, POOL_HIST, WIDTH_B), 1.0),
        "mem_prompt": nrm(ks[5], (BATCH, N_MEM, D_MODEL), 1.0),
        "g_mix": gain(ks[6], (DEPTH, D_MODEL)),
        "w_in": nrm(ks[7], (DEPTH, D_MODEL, PROJ_WIDTH), D_MODEL ** -0.5),
        "g_v": gain(ks[8], (DEPTH, WIDTH_A)),
        "w_s": nrm(ks[9], (DEPTH, HEADS_A, CHUNK, CHUNK), CHUNK ** -0.5),
        "b_s": 1.0 + 0.1 * jax.random.normal(ks[10], (DEPTH, HEADS_A, CHUNK), f32),
        "w_pool": nrm(ks[11], (DEPTH, POOL_GROUPS, POOL_GROUP_DIM, POOL_GROUP_DIM), POOL_GROUP_DIM ** -0.5),
        "s_pool": 1.0 + 0.1 * jax.random.normal(ks[12], (DEPTH, WIDTH_B), f32),
        "w_out": nrm(ks[13], (DEPTH, MIX_WIDTH, D_MODEL), MIX_WIDTH ** -0.5),
        "g_mem": gain(ks[14], (D_MODEL,)),
        "g_xattn": gain(ks[15], (DEPTH, D_MODEL)),
        "w_xq": nrm(ks[16], (DEPTH, D_MODEL, D_MODEL), D_MODEL ** -0.5),
        "w_xk": nrm(ks[17], (DEPTH, D_MODEL, D_MODEL), D_MODEL ** -0.5),
        "w_xv": nrm(ks[18], (DEPTH, D_MODEL, D_MODEL), D_MODEL ** -0.5),
        "w_xo": nrm(ks[19], (DEPTH, D_MODEL, D_MODEL), D_MODEL ** -0.5),
        "g_ffn": gain(ks[20], (DEPTH, D_MODEL)),
        "w_group": nrm(ks[21], (DEPTH, D_MODEL, N_EXPERT_GROUPS), D_MODEL ** -0.5),
        "b_group": nrm(ks[22], (DEPTH, N_EXPERT_GROUPS), 0.01),
        "w_router": nrm(ks[23], (DEPTH, D_MODEL, N_EXPERTS), D_MODEL ** -0.5),
        "b_router": nrm(ks[24], (DEPTH, N_EXPERTS), 0.01),
        "w_gate": nrm(ks[25], (DEPTH, N_EXPERTS, D_MODEL, D_EXPERT), D_MODEL ** -0.5),
        "w_up": nrm(ks[26], (DEPTH, N_EXPERTS, D_MODEL, D_EXPERT), D_MODEL ** -0.5),
        "w_down": nrm(ks[27], (DEPTH, N_EXPERTS, D_EXPERT, D_MODEL), D_EXPERT ** -0.5),
        "g_final": gain(ks[28], (D_MODEL,)),
    }

def reference(x_prompt, x_sample, cache_mem_k, cache_mem_v, state_pool, mem_prompt,
              g_mix, w_in, g_v, w_s, b_s, w_pool, s_pool, w_out,
              g_mem, g_xattn, w_xq, w_xk, w_xv, w_xo,
              g_ffn, w_group, b_group, w_router, b_router, w_gate, w_up, w_down, g_final):
    bp = x_prompt.shape[0]
    mem_n = rmsnorm(mem_prompt, g_mem)
    pool_zero = jnp.zeros((bp, POOL_HIST, WIDTH_B), x_prompt.dtype)
    yp, ys = x_prompt, x_sample
    mk_p, mv_p, cv_p, cv_s, pl_p, pl_s = [], [], [], [], [], []
    for l in range(DEPTH):
        mk = (mem_n @ w_xk[l]).reshape(bp, N_MEM, X_HEADS, X_HEAD_DIM)
        mv = (mem_n @ w_xv[l]).reshape(bp, N_MEM, X_HEADS, X_HEAD_DIM)
        wl = (g_mix[l], w_in[l], g_v[l], w_s[l], b_s[l], w_pool[l], s_pool[l], w_out[l],
              g_xattn[l], w_xq[l], w_xo[l],
              g_ffn[l], w_group[l], b_group[l], w_router[l], b_router[l], w_gate[l], w_up[l], w_down[l])
        yp, cvp, plp = layer_fwd(yp, 0, pool_zero, mk, mv, *wl)
        ys, cvs, pls = layer_fwd(ys, PAST_LEN, state_pool[l], cache_mem_k[l], cache_mem_v[l], *wl)
        mk_p.append(mk)
        mv_p.append(mv)
        cv_p.append(cvp)
        cv_s.append(cvs)
        pl_p.append(plp)
        pl_s.append(pls)
    y_prompt = rmsnorm(yp, g_final)
    y_sample = rmsnorm(ys, g_final)
    return (y_prompt, y_sample, jnp.stack(mk_p), jnp.stack(mv_p), jnp.stack(cv_p), jnp.stack(cv_s),
            jnp.stack(pl_p), jnp.stack(pl_s))


_drawn_inputs = setup_inputs


def setup_inputs(seed=0):
    import zlib

    import numpy as np

    out = dict(_drawn_inputs(seed))
    spreads = {}
    factors = {'g_v': 2.954,
     'g_mem': 2.868,
     'g_xattn': 8.0,
     'b_group': 3.159,
     'b_router': 27.114,
     'g_final': 7.476,
     'g_ffn': 2.992}
    for name, (base, spread) in spreads.items():
        noise = np.random.default_rng([zlib.crc32(name.encode()), seed]).standard_normal(out[name].shape)
        drawn = base * np.exp(spread * noise) if base else spread * noise
        out[name] = __import__('jax').numpy.asarray(drawn.astype(out[name].dtype))
    for name, factor in factors.items():
        out[name] = (out[name] * factor).astype(out[name].dtype)
    return out
```

```python
from contextlib import ExitStack

import numpy as np
import concourse.bass as bass
from concourse import mybir

F32 = mybir.dt.float32
I32 = mybir.dt.int32
BF16 = mybir.dt.bfloat16
ALU = mybir.AluOpType
ACT = mybir.ActivationFunctionType
AX_X = mybir.AxisListType.X
ds = bass.ds

P = 128
D = 1024
KC = D // P
SEQ = 1024
NB, NL = 8, 8
ROWS_S = NB * NL
NT = SEQ // P + 1
TS = NT - 1
WA = 512
HA, DHA = 8, 64
WINDOWS = (2, 4, 8, 16)
NG = len(WINDOWS)
HIST = max(WINDOWS) - 1
NM = 256
MC = NM // P
XH, XD = 4, 256
DC = XD // P
EG, EE = 4, 4
NE = EG * EE
FE = 256
FC = FE // P
EPS = 1e-6
PAIRS = 2 * (SEQ + ROWS_S)
NTILE = (PAIRS + NE * (P - 1)) // P
ESZ = KC * 2 * FE + FC * D
NL2 = EG + NE


def banded():
    main = np.zeros((3, P, NG, P), np.float32)
    prev = np.zeros((2, P, NG, P), np.float32)
    for g, w in enumerate(WINDOWS):
        for t in range(P):
            for k in range(w):
                if t - k >= 0:
                    main[0, t - k, g, t] = 1.0 / min(w, t + 1)
                    main[1, t - k, g, t] = 1.0 / w
                else:
                    prev[0, P + t - k, g, t] = 1.0 / w
            main[0, t, g, t] -= 1.0
            main[1, t, g, t] -= 1.0
        for b in range(NB):
            for l in range(NL):
                for k in range(w):
                    if l - k >= 0:
                        main[2, b * NL + l - k, g, b * NL + l] = 1.0 / w
                    else:
                        prev[1, b * HIST + HIST + l - k, g, b * NL + l] = 1.0 / w
                main[2, b * NL + l, g, b * NL + l] -= 1.0
    return main, prev


class Sems:
    def __init__(self, nc, ctx, tag):
        self.nc, self.ctx, self.tag = nc, ctx, tag

    def __call__(self, name, n=None):
        if n is None:
            return self.ctx.enter_context(self.nc.semaphore(f"{self.tag}_{name}"))
        return [self(f"{name}{i}") for i in range(n)]


def steps(eng, emit, count, lo, hi):
    for s in range(lo):
        emit(s, s)
    with eng.Fori(0, (hi - lo) // 2) as i:
        for u in range(2):
            emit(2 * i + (lo + u), lo + u)
    for s in range(hi, count):
        emit(s, s)


def bcast(ap, n):
    return ap.rearrange("p (a o) -> p a o", o=1).to_broadcast([ap.shape[0], ap.shape[1], n])


def memory_block(nc, io, keep):
    with ExitStack() as ctx:
        sem = Sems(nc, ctx, "m")
        sb = lambda n, s, d=F32: ctx.enter_context(nc.sbuf_tensor("m_" + n, s, d))
        wv = sb("wv", [P, KC, D])
        wk = keep["wkq"]
        xin = sb("xin", [P, MC, D])
        xs = sb("xs", [P, MC, D])
        hT = sb("hT", [P, MC, KC, P])
        knat = sb("knat", [P, MC, D])
        junk = sb("junk", [P, D], BF16)
        st = sb("st", [P, 4 * MC])
        ps, ident, nhalf = keep["ps"], keep["ident"], keep["nhalf"]
        x_ld, wk_ld, wv_ld, c_ld, win_ld = sem("x_ld", MC), sem("wk_ld"), sem("wv_ld"), sem("c_ld"), keep["win_ld"]
        id_ok, sq_ok, r_ok, mean_ok, xs_ok = sem("id_ok"), sem("sq_ok"), sem("r_ok"), sem("mean_ok"), sem("xs_ok")
        tr_ok, hT_ok, k_ps, v_ps, kn_ok, vn_ok = (sem(n) for n in ("tr_ok", "hT_ok", "k_ps", "v_ps", "kn_ok", "vn_ok"))
        kT_ps, kT_ok, out_st = sem("kT_ps"), sem("kT_ok"), sem("out_st")
        block = ctx.enter_context(nc.Block())

        @block.sync
        def _(sp):
            for m in range(MC):
                sp.dma_start(xin[:, m, :], io["mem"][m * P:(m + 1) * P, :]).then_inc(x_ld[m], 16)
            sp.dma_start(keep["gcol"][:, :], io["gcol"]).then_inc(c_ld, 16)
            sp.dma_start(wk[:, :, :], io["w_xk"]).then_inc(wk_ld, 16)
            sp.dma_start(wv[:, :, :], io["w_xv"]).then_inc(wv_ld, 16)
            sp.dma_start(keep["w_in"][:, :, :], io["w_in"]).then_inc(win_ld, 16)
            for m in range(MC):
                sp.wait_ge(kn_ok, 2 * (m + 1))
                sp.dma_start(io["mem_k"][m * P:(m + 1) * P, :], knat[:, m, :]).then_inc(out_st, 16)
            for m in range(MC):
                sp.wait_ge(vn_ok, 2 * (m + 1))
                sp.dma_start(io["mem_v"][m * P:(m + 1) * P, :], keep["V"][:, m, :]).then_inc(out_st, 16)
            sp.wait_ge(out_st, 16 * 2 * MC)

        @block.gpsimd
        def _(pool):
            pool.memset(ident[:, :], 0.0).then_inc(id_ok, 1)
            pool.memset(nhalf[:, :], -0.5).then_inc(id_ok, 1)
            pool.wait_ge(id_ok, 2)
            pool.affine_select(out=ident[:, :], in_=ident[:, :], compare_op=ALU.not_equal, fill=1.0, base=0,
                               pattern=[[-1, P]], channel_multiplier=1).then_inc(id_ok, 1)
            for m in range(MC):
                pool.wait_ge(sq_ok, m + 1)
                pool.tensor_scalar(st[:, 4 * m + 1:4 * m + 2], st[:, 4 * m:4 * m + 1], 1.0 / D, EPS, ALU.mult,
                                   ALU.add).then_inc(mean_ok, 1)
                pool.wait_ge(mean_ok, m + 1)
                pool.tensor_tensor(st[:, 4 * m + 2:4 * m + 3], st[:, 4 * m + 1:4 * m + 2], nhalf[:, :],
                                   ALU.pow).then_inc(r_ok, 1)

        @block.scalar
        def _(act):
            for m in range(MC):
                act.wait_ge(x_ld[m], 16)
                if m:
                    act.wait_ge(sq_ok, m)
                act.activation(junk[:, :], xin[:, m, :], ACT.Square, accum_out=st[:, 4 * m:4 * m + 1]).then_inc(sq_ok, 1)
            for m in range(MC):
                for h in range(2):
                    act.wait_ge(k_ps, 2 * m + h + 1)
                    act.copy(knat[:, m, h * 512:(h + 1) * 512], ps[:, 2 + 2 * m + h, :]).then_inc(kn_ok, 1)
            for m in range(MC):
                for h in range(2):
                    act.wait_ge(v_ps, 2 * m + h + 1)
                    bank = (6, 7, 2, 3)[2 * m + h]
                    act.copy(keep["V"][:, m, h * 512:(h + 1) * 512], ps[:, bank, :]).then_inc(vn_ok, 1)

        @block.vector
        def _(dve):
            dve.wait_ge(c_ld, 16)
            for m in range(MC):
                dve.wait_ge(r_ok, m + 1)
                dve.tensor_scalar(xs[:, m, :], xin[:, m, :], st[:, 4 * m + 2:4 * m + 3], None, ALU.mult).then_inc(xs_ok, 1)
            for m in range(MC):
                dve.wait_ge(tr_ok, m + 1)
                dve.tensor_tensor(hT[:, m, :, :], ps[:, 0:2, :].rearrange("p b (c t) -> p (b c) t", t=P),
                                  bcast(keep["gcol"][:, 0:KC], P), ALU.mult).then_inc(hT_ok, 1)
            for m in range(MC):
                dve.wait_ge(kT_ps, m + 1)
                dve.tensor_copy(keep["KT"][:, :, m * P:(m + 1) * P],
                                ps[:, 4:6, :].rearrange("p b (c t) -> p (b c) t", t=P)).then_inc(kT_ok, 1)

        @block.tensor
        def _(pe):
            pe.wait_ge(id_ok, 3)
            for m in range(MC):
                pe.wait_ge(xs_ok, m + 1)
                if m:
                    pe.wait_ge(hT_ok, m)
                for c in range(KC):
                    last = pe.transpose(ps[:, c // 4, c % 4 * P:(c % 4 + 1) * P], xs[:, m, c * P:(c + 1) * P], ident[:, :])
                last.then_inc(tr_ok, 1)

            def project(w, banks, done):
                for m in range(MC):
                    pe.wait_ge(hT_ok, m + 1)
                    for h in range(2):
                        for c in range(KC):
                            last = pe.matmul(ps[:, banks[2 * m + h], :], hT[:, m, c, :], w[:, c, h * 512:(h + 1) * 512],
                                             start=(c == 0), stop=(c == KC - 1))
                        last.then_inc(done, 1)

            pe.wait_ge(wk_ld, 16)
            project(wk, (2, 3, 4, 5), k_ps)
            pe.wait_ge(wv_ld, 16)
            pe.wait_ge(kn_ok, 2)
            project(wv, (6, 7, 2, 3), v_ps)
            pe.wait_ge(kn_ok, 4)
            for m in range(MC):
                if m:
                    pe.wait_ge(kT_ok, m)
                for c in range(KC):
                    last = pe.transpose(ps[:, 4 + c // 4, c % 4 * P:(c % 4 + 1) * P], knat[:, m, c * P:(c + 1) * P],
                                        ident[:, :])
                last.then_inc(kT_ps, 1)


def mixing_block(nc, io, keep, x1_dram):
    with ExitStack() as ctx:
        sem = Sems(nc, ctx, "a")
        sb = lambda n, s, d=F32: ctx.enter_context(nc.sbuf_tensor("a_" + n, s, d))
        w_in, ps, ident, nhalf = keep["w_in"], keep["ps"], keep["ident"], keep["nhalf"]
        w_out = sb("w_out", [P, KC, D])
        wsT = sb("wsT", [P, HA, P])
        wsTs = sb("wsTs", [ROWS_S, HA, ROWS_S])
        band = sb("band", [P, 3, NG, P])
        bandp = sb("bandp", [P, 2, NG, P])
        w_pool = sb("w_pool", [P, NG, P])
        gv = sb("gv", [P, WA])
        bias = sb("bias", [HA, P + ROWS_S])
        head_of = sb("head_of", [HA, WA])
        hist = sb("hist", [P, WA])
        xin = sb("xin", [P, 2, D])
        xr = sb("xr", [P, 2, D])
        xs = sb("xs", [P, 2, D])
        hT = [sb(f"hT{i}", [P, KC, P]) for i in range(2)]
        z = [sb(f"z{i}", [P, WA]) for i in range(2)]
        u, vg, vn, a, poolT = (sb(n, [P, WA]) for n in ("u", "vg", "vn", "a", "poolT"))
        catT = sb("catT", [P, KC, P])
        junk, junkv = sb("junk", [P, D], BF16), sb("junkv", [P, WA], BF16)
        st = sb("st", [P, 16])
        gmix, spool = keep["gcol"][:, KC:2 * KC], keep["gcol"][:, 4 * KC:4 * KC + NG]
        win_ld = keep["win_ld"]
        wout_ld, mix_ld, x_ld, xr_ld, x1_st = sem("wout_ld"), sem("mix_ld"), sem("x_ld", 2), sem("xr_ld", 2), sem("x1_st", 2)
        (mask_ok, sq_ok, mean_ok, r_ok, xs_ok, tr_ps, hT_ok, v_ps, z_ps, u_ps, vg_ok, vsq_ok, vmean_ok, vr_ok, vn_ok, z_ok,
         u_ok, pool_ps, mix_ps, poolT_ok, a_ok, y_ps, aT_ps, y_ok, aT_ok, out_ps, x1_ok, out_st) = (
            sem(n) for n in ("mask_ok", "sq_ok", "mean_ok", "r_ok", "xs_ok", "tr_ps", "hT_ok", "v_ps", "z_ps", "u_ps",
                             "vg_ok", "vsq_ok", "vmean_ok", "vr_ok", "vn_ok", "z_ok", "u_ok", "pool_ps", "mix_ps",
                             "poolT_ok", "a_ok", "y_ps", "aT_ps", "y_ok", "aT_ok", "out_ps", "x1_ok", "out_st"))
        wkq_ld, state_st = keep["wkq_ld"], sem("state_st")
        consts = [(wsT[:, :, :], io["wsT"]), (wsTs[:, :, :], io["wsTs"]), (band[:, :, :, :], io["band"]),
                  (bandp[:, :, :, :], io["bandp"]), (w_pool[:, :, :], io["w_pool"]),
                  (gv[:, :], io["g_v"].to_broadcast([P, WA])), (bias[:, :], io["bias"]), (head_of[:, :], io["head_of"]),
                  (hist[:, :], io["hist"])]
        block = ctx.enter_context(nc.Block())

        @block.sync
        def _(sp):
            def load_x(t, like):
                if like >= 2:
                    sp.wait_ge(xs_ok, t - 1)
                sp.dma_start(xin[:, like % 2, :], io["x"][ds(t * P, P), :]).then_inc(x_ld[like % 2], 16)

            def load_xr(t, like):
                if like >= 2:
                    sp.wait_ge(x1_st[like % 2], 8 * (t - like % 2))
                sp.dma_start(xr[:, like % 2, :], io["x"][ds(t * P, P), :]).then_inc(xr_ld[like % 2], 16)

            load_x(0, 0)
            load_x(1, 1)
            for dst, src in consts:
                sp.dma_start(dst, src).then_inc(mix_ld, 16)
            sp.dma_start(w_out[:, :, :], io["w_out"]).then_inc(wout_ld, 16)
            load_xr(0, 0)
            sp.dma_start(keep["wkq"][:, :, :], io["w_xq"]).then_inc(wkq_ld, 16)
            sp.dma_start(io["pool_s"][:, 0:HIST - NL, :], io["state"][:, NL:HIST, :]).then_inc(state_st, 16)

            def step(s, like):
                if like + 2 < NT:
                    load_x(s + 2, like + 2)
                if like >= 1:
                    sp.wait_ge(x1_ok, 2 * s)
                    sp.dma_start(x1_dram[ds((s - 1) * P, P), :], xr[:, (like - 1) % 2, :]).then_inc(x1_st[(like - 1) % 2], 16)
                if like + 1 < NT:
                    load_xr(s + 1, like + 1)
            steps(sp, step, NT + 1, 2, 6)
            sp.wait_ge(x1_st[0], 16 * 5)
            sp.wait_ge(x1_st[1], 16 * 4)
            sp.wait_ge(out_st, 16 * 4)
            sp.wait_ge(state_st, 16)

        @block.gpsimd
        def _(pool):
            pool.wait_ge(mix_ld, 16 * len(consts))
            pool.affine_select(out=wsT[:, :, :], in_=wsT[:, :, :], compare_op=ALU.is_ge, fill=0.0, base=0,
                               pattern=[[0, HA], [1, P]], channel_multiplier=-1).then_inc(mask_ok, 1)
            pool.affine_select(out=wsTs[:, :, :], in_=wsTs[:, :, :], compare_op=ALU.is_ge, fill=0.0, base=0,
                               pattern=[[0, HA], [1, ROWS_S]], channel_multiplier=-1).then_inc(mask_ok, 1)

            def x_rms(t, like):
                c = 4 * (like % 2)
                pool.wait_ge(sq_ok, t + 1)
                pool.tensor_scalar(st[:, c + 1:c + 2], st[:, c:c + 1], 1.0 / D, EPS, ALU.mult, ALU.add).then_inc(mean_ok, 1)
                pool.wait_ge(mean_ok, t + 1)
                if like >= 2:
                    pool.wait_ge(xs_ok, t - 1)
                pool.tensor_tensor(st[:, c + 2:c + 3], st[:, c + 1:c + 2], nhalf[:, :], ALU.pow).then_inc(r_ok, 1)

            x_rms(0, 0)
            x_rms(1, 1)

            def step(s, like):
                if like + 2 < NT:
                    x_rms(s + 2, like + 2)
                if like < NT:
                    pool.wait_ge(vsq_ok, s + 1)
                    pool.tensor_scalar(st[:, 9:10], st[:, 8:9], 1.0 / WA, EPS, ALU.mult, ALU.add).then_inc(vmean_ok, 1)
                    pool.wait_ge(vmean_ok, s + 1)
                    if like >= 1:
                        pool.wait_ge(vn_ok, s)
                    pool.tensor_tensor(st[:, 10:11], st[:, 9:10], nhalf[:, :], ALU.pow).then_inc(vr_ok, 1)
                if like == TS - 1:
                    pool.wait_ge(vn_ok, s + 1)
                    pool.dma_start(io["chunk_v_p"], vn[:, :]).then_inc(out_st, 16)
                    pool.wait_ge(z_ok, s + 1)
                    pool.dma_start(io["pool_p"], z[(TS - 1) % 2][P - HIST:P, :]).then_inc(out_st, 16)
                if like == TS:
                    pool.wait_ge(vn_ok, s + 1)
                    pool.dma_start(io["chunk_v_s"], vn[0:ROWS_S, :]).then_inc(out_st, 16)
                    pool.wait_ge(z_ok, s + 1)
                    pool.dma_start(io["pool_s"][:, HIST - NL:HIST, :], z[TS % 2][0:ROWS_S, :]).then_inc(out_st, 16)
            for s in range(NT):
                step(s, s)

        @block.scalar
        def _(act):
            def square(t, like):
                act.wait_ge(x_ld[like % 2], 8 * (t - like % 2) + 16)
                if like >= 1:
                    act.wait_ge(sq_ok, t)
                if like >= 2:
                    act.wait_ge(mean_ok, t - 1)
                act.activation(junk[:, :], xin[:, like % 2, :], ACT.Square,
                               accum_out=st[:, 4 * (like % 2):4 * (like % 2) + 1]).then_inc(sq_ok, 1)

            square(0, 0)
            square(1, 1)

            def step(s, like):
                if like >= 1:
                    act.wait_ge(pool_ps, s)
                    if like >= 2:
                        act.wait_ge(y_ps, s - 1)
                    act.copy(poolT[:, :], ps[:, 6, :]).then_inc(poolT_ok, 1)
                if like + 2 < NT:
                    square(s + 2, like + 2)
                if like < NT:
                    act.wait_ge(v_ps, s + 1)
                    if like >= 1:
                        act.wait_ge(vn_ok, s)
                    act.activation(vg[:, :], ps[:, 3, :], ACT.Gelu_apprx_tanh).then_inc(vg_ok, 1)
                    act.wait_ge(vg_ok, s + 1)
                    if like >= 1:
                        act.wait_ge(vmean_ok, s)
                    act.activation(junkv[:, :], vg[:, :], ACT.Square, accum_out=st[:, 8:9]).then_inc(vsq_ok, 1)
                if like >= 1:
                    act.wait_ge(aT_ps, s)
                    if like >= 2:
                        act.wait_ge(out_ps, 2 * s - 2)
                    act.copy(catT[:, 0:KC // 2, :], ps[:, 5, :].rearrange("p (c t) -> p c t", t=P)).then_inc(aT_ok, 1)
                if like < NT:
                    act.wait_ge(u_ps, s + 1)
                    if like >= 1:
                        act.wait_ge(a_ok, s)
                    act.activation(u[:, :], ps[:, 2, :], ACT.Gelu_apprx_tanh).then_inc(u_ok, 1)
            steps(act, step, NT + 1, 2, 6)

        @block.vector
        def _(dve):
            def scale(t, like):
                dve.wait_ge(r_ok, t + 1)
                if like >= 2:
                    dve.wait_ge(tr_ps, t - 1)
                dve.tensor_scalar(xs[:, like % 2, :], xin[:, like % 2, :], st[:, 4 * (like % 2) + 2:4 * (like % 2) + 3], None,
                                  ALU.mult).then_inc(xs_ok, 1)

            def read_hT(t, like):
                dve.wait_ge(tr_ps, t + 1)
                if like >= 2:
                    dve.wait_ge(u_ps, t - 1)
                dve.tensor_tensor(hT[like % 2][:, :, :], ps[:, 0:2, :].rearrange("p b (c t) -> p (b c) t", t=P),
                                  bcast(gmix, P), ALU.mult).then_inc(hT_ok, 1)

            scale(0, 0)
            scale(1, 1)
            read_hT(0, 0)

            def step(s, like):
                if like >= 1:
                    dve.wait_ge(mix_ps, s)
                    dve.wait_ge(u_ok, s)
                    if like >= 2:
                        dve.wait_ge(aT_ps, s - 1)
                    dve.tensor_tensor(a[:, :], u[:, :], ps[:, 5, :], ALU.mult).then_inc(a_ok, 1)
                if like + 2 < NT:
                    scale(s + 2, like + 2)
                if like + 1 < NT:
                    read_hT(s + 1, like + 1)
                if like >= 1:
                    dve.wait_ge(y_ps, s)
                    if like >= 2:
                        dve.wait_ge(out_ps, 2 * s - 2)
                    dve.tensor_tensor(catT[:, KC // 2:KC, :], ps[:, 6, :].rearrange("p (c t) -> p c t", t=P),
                                      bcast(spool, P), ALU.mult).then_inc(y_ok, 1)
                if like < NT:
                    if like == TS:
                        dve.wait_ge(out_st, 16 * 2)
                    dve.wait_ge(vr_ok, s + 1)
                    if like >= 1:
                        dve.wait_ge(mix_ps, s)
                    dve.scalar_tensor_tensor(out=vn[:, :], in0=vg[:, :], scalar=st[:, 10:11], in1=gv[:, :],
                                             op0=ALU.mult, op1=ALU.mult).then_inc(vn_ok, 1)
                    dve.wait_ge(z_ps, s + 1)
                    if like >= 2:
                        dve.wait_ge(pool_ps, s)
                    dve.tensor_copy(z[like % 2][:, :], ps[:, 4, :]).then_inc(z_ok, 1)
                if like >= 1:
                    if like == 1:
                        dve.wait_ge(xr_ld[0], 16)
                    else:
                        par = (like - 1) % 2
                        dve.wait_ge(xr_ld[par], 8 * (s - 1 - par) + 16)
                    for h in range(2):
                        dve.wait_ge(out_ps, 2 * s - 1 + h)
                        half = xr[:, (like - 1) % 2, h * 512:(h + 1) * 512]
                        dve.tensor_tensor(half, half, ps[:, 7 if h == 0 else 5, :], ALU.add).then_inc(x1_ok, 1)
            dve.wait_ge(mix_ld, 16 * len(consts))
            steps(dve, step, NT + 1, 2, 6)

        @block.tensor
        def _(pe):
            def turn(t, like):
                pe.wait_ge(xs_ok, t + 1)
                if like >= 1:
                    pe.wait_ge(hT_ok, t)
                for c in range(KC):
                    last = pe.transpose(ps[:, c // 4, c % 4 * P:(c % 4 + 1) * P], xs[:, like % 2, c * P:(c + 1) * P],
                                        ident[:, :])
                last.then_inc(tr_ps, 1)

            def project(s, like, bank, col, done):
                for c in range(KC):
                    last = pe.matmul(ps[:, bank, :], hT[like % 2][:, c, :], w_in[:, c, col:col + WA],
                                     start=(c == 0), stop=(c == KC - 1))
                last.then_inc(done, 1)

            def mix(t, like):
                pe.wait_ge(z_ok, t + 1)
                if like >= 1:
                    pe.wait_ge(y_ok, t)
                var = 0 if like == 0 else 2 if like == TS else 1
                before = None if like == 0 else hist if like == TS else z[(like - 1) % 2]
                for g in range(NG):
                    cols = slice(g * P, (g + 1) * P)
                    last = pe.matmul(ps[:, 6, cols], z[like % 2][:, cols], band[:, var, g, :], start=True,
                                     stop=before is None)
                    if before is not None:
                        last = pe.matmul(ps[:, 6, cols], before[:, cols], bandp[:, 0 if like < TS else 1, g, :],
                                         start=False, stop=True)
                last.then_inc(pool_ps, 1)
                pe.wait_ge(vn_ok, t + 1)
                if like >= 1:
                    pe.wait_ge(x1_ok, 2 * t)
                rows = P if like < TS else ROWS_S
                wt, b0 = (wsT, 0) if like < TS else (wsTs, P)
                pe.matmul(ps[0:rows, 5, :], bias[:, b0:b0 + rows], head_of[:, :], start=True, stop=False,
                          skip_group_check=True)
                for h in range(HA):
                    last = pe.matmul(ps[0:rows, 5, h * DHA:(h + 1) * DHA], wt[0:rows, h, 0:rows],
                                     vn[0:rows, h * DHA:(h + 1) * DHA], start=False, stop=(h == HA - 1),
                                     skip_group_check=True)
                last.then_inc(mix_ps, 1)

            def turn_mixed(t, like):
                pe.wait_ge(poolT_ok, t + 1)
                for g in range(NG):
                    last = pe.matmul(ps[:, 6, g * P:(g + 1) * P], w_pool[:, g, :], poolT[:, g * P:(g + 1) * P],
                                     start=True, stop=True)
                last.then_inc(y_ps, 1)
                pe.wait_ge(a_ok, t + 1)
                for c in range(WA // P):
                    last = pe.transpose(ps[:, 5, c * P:(c + 1) * P], a[:, c * P:(c + 1) * P], ident[:, :])
                last.then_inc(aT_ps, 1)

            def out(t, like):
                pe.wait_ge(aT_ok, t + 1)
                pe.wait_ge(y_ok, t + 1)
                for h in range(2):
                    if h == 0 and like >= 1:
                        pe.wait_ge(x1_ok, 2 * t)
                    for c in range(KC):
                        last = pe.matmul(ps[:, 7 if h == 0 else 5, :], catT[:, c, :], w_out[:, c, h * 512:(h + 1) * 512],
                                         start=(c == 0), stop=(c == KC - 1))
                    last.then_inc(out_ps, 1)

            turn(0, 0)
            pe.wait_ge(mix_ld, 16 * len(consts))
            pe.wait_ge(mask_ok, 2)
            pe.wait_ge(win_ld, 16)

            def step(s, like):
                if like >= 1:
                    mix(s - 1, like - 1)
                if like + 1 < NT:
                    turn(s + 1, like + 1)
                if like < NT:
                    pe.wait_ge(hT_ok, s + 1)
                    if like >= 1:
                        pe.wait_ge(vg_ok, s)
                    project(s, like, 3, WA, v_ps)
                if like >= 1:
                    turn_mixed(s - 1, like - 1)
                if like < NT:
                    if like >= 1:
                        pe.wait_ge(z_ok, s)
                    project(s, like, 4, 2 * WA, z_ps)
                    if like >= 1:
                        pe.wait_ge(u_ok, s)
                    project(s, like, 2, 0, u_ps)
                if like >= 1:
                    if like == 1:
                        pe.wait_ge(wout_ld, 16)
                    out(s - 1, like - 1)
            steps(pe, step, NT + 1, 2, 6)


def attention_plan():
    pairs = TS // 2
    plan = [("th", 0), ("qs",), ("th", 1), ("th", 2)]
    for s in range(pairs + 1):
        items = [("kv", 4 * s + i) for i in range(4)] if s < pairs else []
        if s == pairs // 2:
            plan.append(("tps",))
        if s:
            plan += [("tp", s - 1, 0), ("tp", s - 1, 1)] + [("oT", s - 1, c) for c in range(KC // 2)]
        plan += items[0:1]
        if s < pairs:
            plan += [("q", s, c) for c in range(KC // 2)] + items[1:2] + [("sc", s, 0), ("sc", s, 1)] + items[2:3]
            if s + 1 < pairs:
                plan += [("th", 2 * s + 3), ("th", 2 * s + 4)]
            if s == pairs // 2 - 1:
                plan += items[3:4] + [("ts",)]
        if s:
            plan += [("out", s - 1, j, h) for j in range(2) for h in range(2)]
        if s < pairs and s != pairs // 2 - 1:
            plan += items[3:4]
    plan += [("outs", 0), ("outs", 1)]
    ops, seen, rot = [], {}, 0
    for op in plan:
        kind = op[0]
        seen[kind] = seen.get(kind, 0) + 1
        bank = None
        if kind not in ("th", "tp", "sc"):
            bank, rot = rot, rot + 1
        ops.append((op, seen[kind], bank))
    return ops


def attention_block(nc, io, keep, x1_dram):
    plan = attention_plan()
    PAIR = 2 * P
    SCALE = float(XD) ** -0.5
    with ExitStack() as ctx:
        sem = Sems(nc, ctx, "t")
        sb = lambda n, s, d=F32: ctx.enter_context(nc.sbuf_tensor("t_" + n, s, d))
        w_q, KT, V, X, ps, ident, nhalf = (keep[n] for n in ("wkq", "KT", "V", "x", "ps", "ident", "nhalf"))
        w_o = sb("w_o", [P, KC, D])
        hT, qT, pT, oT = (sb(n, [P, KC, PAIR]) for n in ("hT", "qT", "pT", "oT"))
        E = sb("E", [P, 2, D])
        ring = sb("ring", [P, 3, 2 * D])
        xs = sb("xs", [P, D])
        junk = sb("junk", [P, D], BF16)
        qS, oS = sb("qS", [P, KC, ROWS_S]), sb("oS", [P, KC, ROWS_S])
        sS, ES, pS = (sb(n, [P, 2, NB * XH * NL]) for n in ("sS", "ES", "pS"))
        st = sb("st", [P, 4 * NT])
        sm = sb("sm", [P, 3, 4 * XH])
        gx = keep["gcol"][:, 2 * KC:3 * KC]
        NRING = 3
        xS_ld, x_ld, wo_ld, kv_ld = sem("xS_ld"), sem("x_ld"), sem("wo_ld"), sem("kv_ld", NRING)
        sq_ok, mean_ok, r_ok, xs_ok = (sem(n) for n in ("sq_ok", "mean_ok", "r_ok", "xs_ok"))
        done = {k: sem(k + "_ps") for k in ("th", "qs", "kv", "tps", "tp", "oT", "q", "sc", "ts", "out", "outs")}
        t_ok, rot_ok = sem("t_ok"), sem("rot_ok", 2)
        qS_ok, qT_ok, pT_ok, oT_ok, hT_ok, kv_ok, pS_ok = (
            sem(n) for n in ("qS_ok", "qT_ok", "pT_ok", "oT_ok", "hT_ok", "kv_ok", "pS_ok"))
        max_ok, nb_ok, exp_ok, inv_ok, p_ok = (sem(n) for n in ("max_ok", "nb_ok", "exp_ok", "inv_ok", "p_ok"))
        SOFT = {}
        TPOS = {}
        for op, _, _ in plan:
            if op[0] in ("sc", "ts"):
                SOFT[op] = len(SOFT)
            if op[0] in ("th", "tp"):
                TPOS[op] = len(TPOS)
        tile_of = lambda n: TS if n == 0 else n - 1

        def read_out(eng, which):
            for b in (0, 1):
                uses = [rot for op, _, rot in plan if rot is not None and rot % 2 == b and which(op)]
                if uses:
                    eng.wait_ge(rot_ok[b], max(uses) // 2 + 1)

        block = ctx.enter_context(nc.Block())

        @block.sync
        def _(sp):
            def load_kv(i):
                if i >= NRING:
                    sp.wait_ge(done["kv"], i - NRING + 1)
                src = io["kc"][i] if i < NB else io["vc"][i - NB]
                sp.dma_start(ring[:, i % NRING, :], src).then_inc(kv_ld[i % NRING], 16)
            sp.dma_start(X[:, TS, :], x1_dram[TS * P:NT * P, :]).then_inc(xS_ld, 16)
            for t in range(TS):
                sp.dma_start(X[:, t, :], x1_dram[t * P:(t + 1) * P, :]).then_inc(x_ld, 16)
            for i in range(NRING):
                load_kv(i)
            sp.dma_start(w_o[:, :, :], io["w_xo"]).then_inc(wo_ld, 16)
            for i in range(NRING, 2 * NB):
                load_kv(i)

        @block.gpsimd
        def _(pool):
            for n in range(NT):
                pool.wait_ge(sq_ok, n + 1)
                pool.tensor_scalar(st[:, 4 * n + 1:4 * n + 2], st[:, 4 * n:4 * n + 1], 1.0 / D, EPS, ALU.mult,
                                   ALU.add).then_inc(mean_ok, 1)
                pool.wait_ge(mean_ok, n + 1)
                pool.tensor_tensor(st[:, 4 * n + 2:4 * n + 3], st[:, 4 * n + 1:4 * n + 2], nhalf[:, :],
                                   ALU.pow).then_inc(r_ok, 1)

        @block.scalar
        def _(act):
            def square(n):
                act.wait_ge(xS_ld if n == 0 else x_ld, 16 if n == 0 else 16 * TS)
                if n:
                    act.wait_ge(sq_ok, n)
                act.activation(junk[:, :], X[:, tile_of(n), :], ACT.Square,
                               accum_out=st[:, 4 * n:4 * n + 1]).then_inc(sq_ok, 1)

            def exps(k, cols, out, groups):
                act.wait_ge(nb_ok, k + 1)
                for g in range(groups):
                    last = act.activation(out[:, g * NM:(g + 1) * NM], cols[:, g * NM:(g + 1) * NM], ACT.Exp,
                                          bias=sm[:, 1, 4 * (k % 4) + g:4 * (k % 4) + g + 1], scale=SCALE,
                                          accum_out=sm[:, 2, 4 * (k % 4) + g:4 * (k % 4) + g + 1])
                return last

            square(0)
            square(1)
            for op, n, rot in plan:
                kind = op[0]
                bank = None if rot is None else ps[:, 2 + rot % 2, :]
                if kind == "th" and op[1] + 2 < NT:
                    square(op[1] + 2)
                elif kind == "qs":
                    act.wait_ge(done["qs"], 1)
                    act.copy(qS[:, :, :], bank.rearrange("p (c t) -> p c t", t=ROWS_S)).then_inc(rot_ok[rot % 2], 1)
                elif kind == "q":
                    act.wait_ge(done["q"], n)
                    if op[1]:
                        act.wait_ge(done["sc"], 2 * op[1])
                    act.copy(qT[:, 2 * op[2]:2 * op[2] + 2, :], bank.rearrange("p (c t) -> p c t", t=PAIR)).then_inc(
                        rot_ok[rot % 2], 1)
                elif kind == "kv":
                    act.wait_ge(done["kv"], n)
                    if op[1] < NB:
                        b = op[1]
                        act.copy(sS[:, :, b * 32:(b + 1) * 32], bank[:, 0:64].rearrange("p (m r) -> p m r", m=MC)).then_inc(
                            rot_ok[rot % 2], 1)
                    else:
                        b = op[1] - NB
                        act.copy(oS[:, :, b * NL:(b + 1) * NL], bank[:, 0:64].rearrange("p (c r) -> p c r", r=NL)).then_inc(
                            rot_ok[rot % 2], 1)
                elif kind == "sc":
                    if op[1]:
                        act.wait_ge(done["tp"], 2 * op[1] - 1 + op[2])
                    j = op[2]
                    exps(SOFT[op], ps[:, 4 + 2 * j:6 + 2 * j, :].rearrange("p b n -> p (b n)"), E[:, j, :], XH).then_inc(
                        exp_ok, 1)
                elif kind == "ts":
                    exps(SOFT[op], bank, ES[:, :, :].rearrange("p a n -> p (a n)"), 2).then_inc(exp_ok, 1)
                elif kind == "tps":
                    act.wait_ge(done["tps"], 1)
                    act.copy(pS[:, :, :], bank.rearrange("p (m r) -> p m r", m=MC)).then_inc(rot_ok[rot % 2], 1)

        @block.vector
        def _(dve):
            def scale(n):
                dve.wait_ge(r_ok, n + 1)
                if n:
                    dve.wait_ge(done["th"], n)
                dve.tensor_scalar(xs[:, :], X[:, tile_of(n), :], st[:, 4 * n + 2:4 * n + 3], None, ALU.mult).then_inc(xs_ok, 1)

            def softmax(k, scores, out, groups, wait, ok):
                dve.wait_ge(*wait)
                c = 4 * (k % 4)
                dve.tensor_reduce(sm[:, 0, c:c + groups], scores, AX_X, ALU.max).then_inc(max_ok, 1)
                dve.wait_ge(max_ok, k + 1)
                dve.tensor_scalar(sm[:, 1, c:c + groups], sm[:, 0, c:c + groups], -SCALE, None, ALU.mult).then_inc(nb_ok, 1)
                dve.wait_ge(exp_ok, k + 1)
                dve.reciprocal(sm[:, 0, c:c + groups], sm[:, 2, c:c + groups]).then_inc(inv_ok, 1)
                dve.wait_ge(inv_ok, k + 1)
                return dve.tensor_tensor(out, out, bcast(sm[:, 0, c:c + groups], NM), ALU.mult).then_inc(ok, 1)

            scale(0)
            for op, n, rot in plan:
                kind = op[0]
                bank = None if rot is None else ps[:, 2 + rot % 2, :]
                if kind == "th":
                    i = op[1]
                    dve.wait_ge(done["th"], n)
                    j = 0 if i == 0 else (i - 1) % 2
                    if i in (1, 2):
                        dve.wait_ge(done["qs"], 1)
                    elif i > 2:
                        dve.wait_ge(done["q"], KC // 2 * ((i - 1) // 2))
                    dve.tensor_tensor(hT[:, :, j * P:(j + 1) * P], ps[:, 0:2, :].rearrange("p b (c t) -> p (b c) t", t=P),
                                      bcast(gx, P), ALU.mult).then_inc(t_ok, 1)
                    if i + 1 < NT:
                        scale(i + 1)
                elif kind == "tp":
                    dve.wait_ge(done["tp"], n)
                    s, j = op[1], op[2]
                    if s:
                        dve.wait_ge(done["oT"], KC // 2 * s)
                    dve.tensor_copy(pT[:, :, j * P:(j + 1) * P],
                                    ps[:, 0:2, :].rearrange("p b (c t) -> p (b c) t", t=P)).then_inc(t_ok, 1)
                elif kind == "oT":
                    s, c = op[1], op[2]
                    dve.wait_ge(done["oT"], n)
                    if s:
                        dve.wait_ge(done["out"], 4 * s)
                    dve.tensor_copy(oT[:, 2 * c:2 * c + 2, :], bank.rearrange("p (c t) -> p c t", t=PAIR)).then_inc(
                        rot_ok[rot % 2], 1)
                elif kind == "out":
                    s, j, h = op[1:]
                    dve.wait_ge(done["out"], n)
                    x = X[:, 2 * s + j, h * 512:(h + 1) * 512]
                    dve.tensor_tensor(x, x, bank, ALU.add).then_inc(rot_ok[rot % 2], 1)
                elif kind == "outs":
                    dve.wait_ge(done["outs"], n)
                    x = X[0:ROWS_S, TS, op[1] * 512:(op[1] + 1) * 512]
                    dve.tensor_tensor(x, x, bank[0:ROWS_S, :], ALU.add).then_inc(rot_ok[rot % 2], 1)
                elif kind == "sc":
                    j = op[2]
                    softmax(SOFT[op], ps[:, 4 + 2 * j:6 + 2 * j, :].rearrange("p b (h m) -> p (b h) m", m=NM),
                            E[:, j, :].rearrange("p (h m) -> p h m", m=NM), XH, (done["sc"], n), p_ok)
                elif kind == "ts":
                    softmax(SOFT[op], bank.rearrange("p (a m) -> p a m", m=NM), ES[:, :, :], 2, (done["ts"], 1),
                            rot_ok[rot % 2])

        @block.tensor
        def _(pe):
            for op, n, rot in plan:
                kind = op[0]
                if rot is not None:
                    bank = ps[:, 2 + rot % 2, :]
                    if rot >= 2:
                        pe.wait_ge(rot_ok[rot % 2], rot // 2)
                if kind in ("th", "tp") and TPOS[op]:
                    pe.wait_ge(t_ok, TPOS[op])
                if kind == "th":
                    pe.wait_ge(xs_ok, op[1] + 1)
                    for c in range(KC):
                        last = pe.transpose(ps[:, c // 4, c % 4 * P:(c % 4 + 1) * P], xs[:, c * P:(c + 1) * P], ident[:, :])
                elif kind == "tp":
                    pe.wait_ge(p_ok, 2 * op[1] + op[2] + 1)
                    for c in range(KC):
                        last = pe.transpose(ps[:, c // 4, c % 4 * P:(c % 4 + 1) * P], E[:, op[2], c * P:(c + 1) * P],
                                            ident[:, :])
                elif kind == "qs":
                    pe.wait_ge(keep["wkq_ld"], 16)
                    pe.wait_ge(t_ok, TPOS[("th", 0)] + 1)
                    for c in range(KC):
                        for k in range(KC):
                            last = pe.matmul(bank[:, c * ROWS_S:(c + 1) * ROWS_S], w_q[:, k, c * P:(c + 1) * P],
                                             hT[:, k, 0:ROWS_S], start=(k == 0), stop=(k == KC - 1))
                elif kind == "q":
                    pe.wait_ge(t_ok, TPOS[("th", 2 * op[1] + 2)] + 1)
                    for i in range(2):
                        c = 2 * op[2] + i
                        for k in range(KC):
                            last = pe.matmul(bank[:, i * PAIR:(i + 1) * PAIR], w_q[:, k, c * P:(c + 1) * P], hT[:, k, :],
                                             start=(k == 0), stop=(k == KC - 1))
                elif kind == "sc":
                    s, j = op[1], op[2]
                    read_out(pe, lambda o: o[0] == "q" and o[1] == s)
                    if s:
                        pe.wait_ge(exp_ok, SOFT[("sc", s - 1, j)] + 1)
                    for h in range(XH):
                        for dc in range(DC):
                            last = pe.matmul(ps[:, 4 + 2 * j + h // 2, h % 2 * NM:(h % 2 + 1) * NM],
                                             qT[:, 2 * h + dc, j * P:(j + 1) * P], KT[:, 2 * h + dc, :],
                                             start=(dc == 0), stop=(dc == DC - 1))
                elif kind == "oT":
                    pe.wait_ge(t_ok, TPOS[("tp", op[1], 1)] + 1)
                    for i in range(2):
                        c = 2 * op[2] + i
                        for mc in range(MC):
                            last = pe.matmul(bank[:, i * PAIR:(i + 1) * PAIR], V[:, mc, c * P:(c + 1) * P],
                                             pT[:, c // DC * MC + mc, :], start=(mc == 0), stop=(mc == MC - 1))
                elif kind == "out":
                    s, j, h = op[1:]
                    if (s, j, h) == (0, 0, 0):
                        pe.wait_ge(wo_ld, 16)
                    read_out(pe, lambda o: o[0] == "oT" and o[1] == s)
                    for c in range(KC):
                        last = pe.matmul(bank, oT[:, c, j * P:(j + 1) * P], w_o[:, c, h * 512:(h + 1) * 512],
                                         start=(c == 0), stop=(c == KC - 1))
                elif kind == "kv":
                    i = op[1]
                    pe.wait_ge(kv_ld[i % NRING], 16 * (i // NRING + 1))
                    if i == 0:
                        pe.wait_ge(rot_ok[0], 1)
                    if i < NB:
                        kc = ring[:, i % NRING, :].rearrange("p (c m) -> p c m", c=KC)
                        for mc in range(MC):
                            for h in range(XH):
                                o = (mc * XH + h) * NL
                                for dc in range(DC):
                                    last = pe.matmul(bank[:, o:o + NL], kc[:, 2 * h + dc, mc * P:(mc + 1) * P],
                                                     qS[:, 2 * h + dc, i * NL:(i + 1) * NL],
                                                     start=(dc == 0), stop=(dc == DC - 1))
                    else:
                        b = i - NB
                        if b == 0:
                            read_out(pe, lambda o: o[0] == "tps")
                        vc = ring[:, i % NRING, :].rearrange("p (m n) -> p m n", m=MC)
                        for c in range(KC):
                            o = (b * XH + c // DC) * NL
                            for mc in range(MC):
                                last = pe.matmul(bank[:, c * NL:(c + 1) * NL], vc[:, mc, c * P:(c + 1) * P],
                                                 pS[:, mc, o:o + NL], start=(mc == 0), stop=(mc == MC - 1))
                elif kind == "ts":
                    read_out(pe, lambda o: o[0] == "kv" and o[1] < NB)
                    for mc in range(MC):
                        for rg in range(2):
                            last = pe.transpose(bank[:, rg * NM + mc * P:rg * NM + (mc + 1) * P],
                                                sS[:, mc, rg * P:(rg + 1) * P], ident[:, :])
                elif kind == "tps":
                    read_out(pe, lambda o: o[0] == "ts")
                    for mc in range(MC):
                        for rg in range(2):
                            last = pe.transpose(bank[:, mc * NM + rg * P:mc * NM + (rg + 1) * P],
                                                ES[:, rg, mc * P:(mc + 1) * P], ident[:, :])
                elif kind == "outs":
                    if op[1] == 0:
                        read_out(pe, lambda o: o[0] == "kv" and o[1] >= NB)
                    for c in range(KC):
                        last = pe.matmul(bank[0:ROWS_S, :], oS[:, c, :], w_o[:, c, op[1] * 512:(op[1] + 1) * 512],
                                         start=(c == 0), stop=(c == KC - 1))
                last.then_inc(done[kind], 1)


def routing_block(nc, io, keep, h_dram):
    with ExitStack() as ctx:
        sem = Sems(nc, ctx, "r")
        sb = lambda n, s, d=F32: ctx.enter_context(nc.sbuf_tensor("r_" + n, s, d))
        X, ps, ident, nhalf = keep["x"], keep["ps"], keep["ident"], keep["nhalf"]
        POS, WT, IDX, TEXP, FREE = (keep[n] for n in ("pos", "wt", "idx", "texp", "free"))
        K2 = 2 * NT
        NTHR = NT
        gffn = sb("gffn", [P, D])
        wr = sb("wr", [P, KC, NL2])
        brow = sb("brow", [1, NL2])
        ones = sb("ones", [P, P])
        before = sb("before", [P, P])
        cst = sb("cst", [P, 4 + NTHR + NTILE + P])
        tok = sb("tok", [P, 2, NT])
        xs = sb("xs", [P, 2, D])
        hT = [sb(f"hT{i}", [P, KC, P]) for i in range(2)]
        junk = sb("junk", [P, D], BF16)
        st = sb("st", [P, 4 * NT])
        GL, EL = sb("GL", [P, NT, EG]), sb("EL", [P, NT, EG, EE])
        t4a, t4b, G1, d4, sel, sel2 = (sb(n, [P, NT, 4]) for n in ("t4a", "t4b", "G1", "d4", "sel", "sel2"))
        H = sb("H", [P, 2, NT, EE])
        m = {n: sb(n, [P, NT]) for n in ("gmax", "gsum", "gp", "km", "m1", "m2", "dm", "ex", "den", "rden")}
        prod = sb("prod", [P, NT, EG, EE])
        M = sb("M", [P, 2, NT, NE])
        Ms = sb("Ms", [P, NT, NE])
        tot = sb("tot", [P, NT, NE])
        run = sb("run", [P, NT + 1, NE])
        rank = sb("rank", [P, NT, NE])
        big = sb("big", [P, K2, P])
        cmp9 = sb("cmp9", [P, NE, NTHR])
        tl, ea, eb, base = (sb(n, [P, NE]) for n in ("tl", "ea", "eb", "base"))
        rk, bk, fl, rr, tt, pf = (sb(n, [P, K2]) for n in ("rk", "bk", "fl", "rr", "tt", "pf"))
        cmp8 = sb("cmp8", [P, K2, NTHR - 1])
        A = sb("A", [P, K2, NTILE])
        te = sb("te", [P, NTILE, NE])
        tef = sb("tef", [P, NTILE])
        tef2 = sb("tef2", [P, NTILE])
        ones_ok, c_ld, h_st = sem("ones_ok"), sem("c_ld"), sem("h_st", 2)
        sq_ok, mean_ok, r_ok, xs_ok, tr_ps, hT_ok, lg_ps, lg_ok = (
            sem(n) for n in ("sq_ok", "mean_ok", "r_ok", "xs_ok", "tr_ps", "hT_ok", "lg_ps", "lg_ok"))
        step_ok, gd_ok, ge_ok, dm_ok, ex_ok, M_ok, cnt_ps, AB_ok, idx_ps = (
            sem(n) for n in ("step_ok", "gd_ok", "ge_ok", "dm_ok", "ex_ok", "M_ok", "cnt_ps", "AB_ok", "idx_ps"))
        consts = [(gffn[:, :], io["g_ffn"].to_broadcast([P, D])), (wr[:, :, :], io["w_r"]), (brow[:, :], io["b_r"]),
                  (before[:, :], io["before"]), (cst[:, :], io["cst"].to_broadcast([P, 4 + NTHR + NTILE + P])),
                  (tok[:, :, :], io["tok"])]
        fall4 = cst[:, 0:4]
        thr = cst[:, 4:4 + NTHR]
        itile = cst[:, 4 + NTHR:4 + NTHR + NTILE]
        irow = cst[:, 4 + NTHR + NTILE:]
        block = ctx.enter_context(nc.Block())

        @block.sync
        def _(sp):
            for dst, src in consts:
                sp.dma_start(dst, src).then_inc(c_ld, 16)

            def step(s, like):
                sp.wait_ge(xs_ok, s + 1)
                sp.dma_start(h_dram[ds(s * P, P), :], xs[:, like % 2, :]).then_inc(h_st[like % 2], 16)
            steps(sp, step, NT, 2, 6)
            sp.wait_ge(h_st[0], 16 * 5)
            sp.wait_ge(h_st[1], 16 * 4)

        @block.gpsimd
        def _(pool):
            pool.memset(ones[:, :], 1.0).then_inc(ones_ok, 1)
            for n in range(NT):
                pool.wait_ge(sq_ok, n + 1)
                pool.tensor_scalar(st[:, 4 * n + 1:4 * n + 2], st[:, 4 * n:4 * n + 1], 1.0 / D, EPS, ALU.mult,
                                   ALU.add).then_inc(mean_ok, 1)
                pool.wait_ge(mean_ok, n + 1)
                pool.tensor_tensor(st[:, 4 * n + 2:4 * n + 3], st[:, 4 * n + 1:4 * n + 2], nhalf[:, :],
                                   ALU.pow).then_inc(r_ok, 1)

        @block.scalar
        def _(act):
            for n in range(NT):
                if n:
                    act.wait_ge(sq_ok, n)
                act.activation(junk[:, :], X[:, n, :], ACT.Square, accum_out=st[:, 4 * n:4 * n + 1]).then_inc(sq_ok, 1)
                if n >= 1:
                    act.wait_ge(tr_ps, n)
                    if n >= 3:
                        act.wait_ge(lg_ps, n - 2)
                    act.copy(hT[(n - 1) % 2][:, :, :], ps[:, 0:2, :].rearrange("p b (c t) -> p (b c) t", t=P)).then_inc(
                        hT_ok, 1)
            act.wait_ge(tr_ps, NT)
            act.wait_ge(lg_ps, NT - 2)
            act.copy(hT[(NT - 1) % 2][:, :, :], ps[:, 0:2, :].rearrange("p b (c t) -> p (b c) t", t=P)).then_inc(hT_ok, 1)
            act.wait_ge(gd_ok, 1)
            act.activation(t4b[:, :, :], d4[:, :, :], ACT.Exp).then_inc(ge_ok, 1)
            act.wait_ge(dm_ok, 1)
            act.activation(m["ex"][:, :], m["dm"][:, :], ACT.Exp).then_inc(ex_ok, 1)

        @block.tensor
        def _(pe):
            def logits(n):
                pe.wait_ge(hT_ok, n + 1)
                out = ps[:, 2, n * NL2:(n + 1) * NL2]
                for c in range(KC):
                    pe.matmul(out, hT[n % 2][:, c, :], wr[:, c, :], start=(c == 0), stop=False)
                pe.matmul(out, ones[0:1, :], brow[:, :], start=False, stop=True).then_inc(lg_ps, 1)

            pe.wait_ge(c_ld, 16 * len(consts))
            pe.wait_ge(ones_ok, 1)
            for n in range(NT):
                pe.wait_ge(xs_ok, n + 1)
                if n:
                    pe.wait_ge(hT_ok, n)
                for c in range(KC):
                    last = pe.transpose(ps[:, c // 4, c % 4 * P:(c % 4 + 1) * P], xs[:, n % 2, c * P:(c + 1) * P],
                                        ident[:, :])
                last.then_inc(tr_ps, 1)
                if n:
                    logits(n - 1)
            logits(NT - 1)
            pe.wait_ge(M_ok, 1)
            Mf = Ms[:, :, :].rearrange("p t e -> p (t e)")
            pe.matmul(ps[:, 3, 0:NT * NE], before[:, :], Mf, start=True, stop=True)
            pe.matmul(ps[:, 4, 0:NT * NE], ones[:, :], Mf, start=True, stop=True).then_inc(cnt_ps, 1)
            pe.wait_ge(AB_ok, 1)
            for i in range(K2):
                last = pe.matmul(ps[:, 5, 0:NTILE], big[:, i, :], A[:, i, :], start=(i == 0), stop=(i == K2 - 1))
            last.then_inc(idx_ps, 1)

        @block.vector
        def _(dve):
            dve.wait_ge(c_ld, 16 * len(consts))
            for n in range(NT):
                dve.wait_ge(r_ok, n + 1)
                if n >= 2:
                    dve.wait_ge(tr_ps, n - 1)
                    dve.wait_ge(h_st[n % 2], 16 * (n // 2))
                dve.scalar_tensor_tensor(out=xs[:, n % 2, :], in0=X[:, n, :], scalar=st[:, 4 * n + 2:4 * n + 3],
                                         in1=gffn[:, :], op0=ALU.mult, op1=ALU.mult).then_inc(xs_ok, 1)
            count = [0]

            def then(ins):
                count[0] += 1
                ins.then_inc(step_ok, 1)
                dve.wait_ge(step_ok, count[0])

            v, r = dve.tensor_tensor, dve.tensor_reduce
            dve.wait_ge(lg_ps, NT)
            lg = ps[:, 2, 0:NT * NL2].rearrange("p (t n) -> p t n", n=NL2)
            dve.tensor_copy(EL[:, :, :, :].rearrange("p t g e -> p t (g e)"), lg[:, :, EG:NL2])
            then(dve.tensor_copy(GL[:, :, :], lg[:, :, 0:EG]))
            then(r(m["gmax"][:, :], GL[:, :, :], AX_X, ALU.max))
            v(d4[:, :, :], GL[:, :, :], bcast(m["gmax"][:, :], 4), ALU.subtract).then_inc(gd_ok, 1)
            f4 = fall4.rearrange("p (o n) -> p o n", o=1).to_broadcast([P, NT, 4])

            def first_of(out, x, top):
                then(v(t4a[:, :, :], x, bcast(top, 4), ALU.is_equal))
                then(v(t4a[:, :, :], t4a[:, :, :], f4, ALU.mult))
                then(r(m["km"][:, :], t4a[:, :, :], AX_X, ALU.max))
                then(v(out, t4a[:, :, :], bcast(m["km"][:, :], 4), ALU.is_equal))

            first_of(G1[:, :, :], GL[:, :, :], m["gmax"][:, :])
            dve.wait_ge(ge_ok, 1)
            then(r(m["gsum"][:, :], t4b[:, :, :], AX_X, ALU.add))
            then(dve.reciprocal(m["gp"][:, :], m["gsum"][:, :]))
            g1e = G1[:, :, :].rearrange("p t (g o) -> p t g o", o=1).to_broadcast([P, NT, EG, EE])
            then(v(prod[:, :, :, :], EL[:, :, :, :], g1e, ALU.mult))
            then(r(sel[:, :, :], prod[:, :, :, :].rearrange("p t g e -> p t e g"), AX_X, ALU.add))
            then(r(m["m1"][:, :], sel[:, :, :], AX_X, ALU.max))
            first_of(H[:, 0, :, :], sel[:, :, :], m["m1"][:, :])
            then(dve.scalar_tensor_tensor(out=sel2[:, :, :], in0=H[:, 0, :, :], scalar=-3.0e38, in1=sel[:, :, :],
                                          op0=ALU.mult, op1=ALU.add))
            then(r(m["m2"][:, :], sel2[:, :, :], AX_X, ALU.max))
            first_of(H[:, 1, :, :], sel2[:, :, :], m["m2"][:, :])
            v(m["dm"][:, :], m["m2"][:, :], m["m1"][:, :], ALU.subtract).then_inc(dm_ok, 1)
            dve.wait_ge(ex_ok, 1)
            then(dve.tensor_scalar(m["den"][:, :], m["ex"][:, :], 1.0, None, ALU.add))
            then(dve.reciprocal(m["rden"][:, :], m["den"][:, :]))
            then(v(WT[:, 0, :], m["gp"][:, :], m["rden"][:, :], ALU.mult))
            then(v(WT[:, 1, :], WT[:, 0, :], m["ex"][:, :], ALU.mult))
            then(v(G1[:, :, :], G1[:, :, :], bcast(tok[:, 1, :], 4), ALU.mult))
            for k in range(2):
                for g in range(EG):
                    last = v(M[:, k, :, g * EE:(g + 1) * EE], H[:, k, :, :],
                             G1[:, :, g:g + 1].to_broadcast([P, NT, EE]), ALU.mult)
            then(last)
            v(Ms[:, :, :], M[:, 0, :, :], M[:, 1, :, :], ALU.add).then_inc(M_ok, 1)
            dve.wait_ge(cnt_ps, 1)
            dve.memset(run[:, 0, :], 0.0)
            then(dve.tensor_copy(tot[:, :, :], ps[:, 4, 0:NT * NE].rearrange("p (t e) -> p t e", e=NE)))
            for t in range(NT):
                then(v(run[:, t + 1, :], run[:, t, :], tot[:, t, :], ALU.add))
            then(v(rank[:, :, :], run[:, 0:NT, :], ps[:, 3, 0:NT * NE].rearrange("p (t e) -> p t e", e=NE), ALU.add))
            then(v(cmp9[:, :, :], bcast(run[:, NT, :], NTHR), thr.rearrange("p (o n) -> p o n", o=1).to_broadcast(
                [P, NE, NTHR]), ALU.is_gt))
            then(r(tl[:, :], cmp9[:, :, :], AX_X, ALU.add))
            then(dve.tensor_copy(ea[:, :], tl[:, :]))
            src, dst = ea, eb
            for k in (1, 2, 4, 8):
                dve.tensor_copy(dst[:, 0:k], src[:, 0:k])
                then(v(dst[:, k:NE], src[:, k:NE], src[:, 0:NE - k], ALU.add))
                src, dst = dst, src
            end = src
            then(v(base[:, :], end[:, :], tl[:, :], ALU.subtract))
            then(dve.tensor_scalar(FREE[:, :], end[:, :], 2.0, 2.0, ALU.mult, ALU.add))
            then(v(te[:, :, :], end[:, :].rearrange("p (o e) -> p o e", o=1).to_broadcast([P, NTILE, NE]),
                   bcast(itile, NE), ALU.is_le))
            then(r(tef[:, :], te[:, :, :], AX_X, ALU.add))
            then(dve.tensor_scalar(tef2[:, :], tef[:, :], float(NE - 1), 1.0, ALU.min, ALU.add))
            then(dve.tensor_copy(TEXP[:, 0, :], tef2[:, :]))
            then(dve.tensor_scalar(tef2[:, :], tef[:, :], float(NE - 1), None, ALU.min))
            then(dve.tensor_copy(tef[:, :], tef2[:, :]))
            for k in range(keep["nbuf"], NE, keep["nbuf"]):
                then(dve.tensor_scalar(te[:, :, 0], tef2[:, :], float(k), -float(keep["nbuf"]), ALU.is_ge, ALU.mult))
                then(v(tef[:, :], tef[:, :], te[:, :, 0], ALU.add))
            then(dve.tensor_scalar(tef2[:, :], tef[:, :], float(ESZ), None, ALU.mult))
            then(dve.tensor_copy(TEXP[:, 1, :], tef2[:, :]))
            for k in range(2):
                then(v(prod[:, :, :, :].rearrange("p t g e -> p t (g e)"), M[:, k, :, :], rank[:, :, :], ALU.mult))
                then(r(rk[:, k * NT:(k + 1) * NT], prod[:, :, :, :].rearrange("p t g e -> p t (g e)"), AX_X, ALU.add))
                then(v(prod[:, :, :, :].rearrange("p t g e -> p t (g e)"), M[:, k, :, :],
                       base[:, :].rearrange("p (o e) -> p o e", o=1).to_broadcast([P, NT, NE]), ALU.mult))
                then(r(bk[:, k * NT:(k + 1) * NT], prod[:, :, :, :].rearrange("p t g e -> p t (g e)"), AX_X, ALU.add))
            then(v(cmp8[:, :, :], bcast(rk[:, :], NTHR - 1), thr[:, 1:NTHR].rearrange("p (o n) -> p o n", o=1).to_broadcast(
                [P, K2, NTHR - 1]), ALU.is_ge))
            then(r(fl[:, :], cmp8[:, :, :], AX_X, ALU.add))
            dve.scalar_tensor_tensor(out=rr[:, :], in0=fl[:, :], scalar=-float(P), in1=rk[:, :], op0=ALU.mult, op1=ALU.add)
            then(v(tt[:, :], bk[:, :], fl[:, :], ALU.add))
            then(dve.scalar_tensor_tensor(out=pf[:, :], in0=tt[:, :], scalar=float(P), in1=rr[:, :], op0=ALU.mult,
                                          op1=ALU.add))
            then(dve.tensor_copy(POS[:, :], pf[:, :]))
            v(big[:, :, :], bcast(rr[:, :], P), irow.rearrange("p (o n) -> p o n", o=1).to_broadcast([P, K2, P]),
              ALU.is_equal)
            then(v(A[:, :, :], bcast(tt[:, :], NTILE), itile.rearrange("p (o n) -> p o n", o=1).to_broadcast(
                [P, K2, NTILE]), ALU.is_equal))
            for k in range(2):
                last = v(A[:, k * NT:(k + 1) * NT, :], A[:, k * NT:(k + 1) * NT, :], bcast(tok[:, 0, :], NTILE), ALU.mult)
            last.then_inc(AB_ok, 1)
            dve.wait_ge(idx_ps, 1)
            dve.tensor_copy(IDX[:, :], ps[:, 5, 0:NTILE])


def experts_block(nc, io, keep, h_dram, y_dram):
    NBUF = keep["nbuf"]
    with ExitStack() as ctx:
        sem = Sems(nc, ctx, "e")
        sb = lambda n, s, d=F32: ctx.enter_context(nc.sbuf_tensor("e_" + n, s, d))
        ps, ident, IDX, TEXP, FREE = (keep[n] for n in ("ps", "ident", "idx", "texp", "free"))
        W = sb("W", [P, NBUF * ESZ])
        xg = sb("xg", [P, 2, D])
        xT = [sb(f"xT{i}", [P, KC, P]) for i in range(2)]
        aT = [sb(f"aT{i}", [P, FC, P]) for i in range(2)]
        sg, a = sb("sg", [P, FE]), sb("a", [P, FE])
        y = sb("y", [P, 2, D])
        w_ld, w_ok = sem("w_ld", 2), sem("w_ok")
        x_ld, tr_ps, xT_ok, gu_ps, sg_ok, a_ok, aT_ps, aT_ok, dn_ps, y_ok = (
            sem("x_ld", 2), *(sem(n) for n in ("tr_ps", "xT_ok", "gu_ps", "sg_ok", "a_ok", "aT_ps", "aT_ok",
                                                             "dn_ps", "y_ok")))
        y_st = sem("y_st", 2)
        block = ctx.enter_context(nc.Block())

        @block.sync
        def _(sp):
            def load(e, like):
                if like >= NBUF:
                    end = sp.value_load(FREE[0:1, ds(e - NBUF, 1)], min_val=2, max_val=2 * NTILE + 2)
                    sp.wait_ge(dn_ps, end)
                sp.dma_start(W[:, ds(like % NBUF * ESZ, ESZ)], io["w_e"][ds(e * P, P), :]).then_inc(w_ld[like % 2], 16)

            def arrived(e, like):
                sp.wait_ge(w_ld[like % 2], 8 * (e - like % 2) + 16)
                sp.sem_inc(w_ok, 1)

            for e in range(NBUF):
                load(e, e)
                if e:
                    arrived(e - 1, e - 1)
            with sp.Fori(0, NE // NBUF - 1) as i:
                for u in range(NBUF):
                    load(NBUF * i + (NBUF + u), NBUF + u)
                    arrived(NBUF * i + (NBUF + u - 1), NBUF + u - 1)
            arrived(NE - 1, NE - 1)

        @block.gpsimd
        def _(pool):
            for j in range(NTILE):
                if j >= 2:
                    pool.wait_ge(tr_ps, j - 1)
                pool.indirect_dma_start(xg[:, j % 2, :], None, h_dram[:, :],
                                        bass.IndirectOffsetOnAxis(ap=IDX[:, j:j + 1], axis=0)).then_inc(x_ld[j % 2], 16)

        @block.scalar
        def _(act):
            def step(s, like):
                if like < NTILE:
                    act.wait_ge(tr_ps, s + 1)
                    if like >= 2:
                        act.wait_ge(gu_ps, s - 1)
                    act.copy(xT[like % 2][:, :, :], ps[:, 0:2, :].rearrange("p b (c t) -> p (b c) t", t=P)).then_inc(
                        xT_ok, 1)
                if 1 <= like <= NTILE:
                    act.wait_ge(gu_ps, s)
                    if like >= 2:
                        act.wait_ge(a_ok, s - 1)
                    act.activation(sg[:, :], ps[:, 2 + (like - 1) % 2, 0:FE], ACT.Silu).then_inc(sg_ok, 1)
                if like >= 2:
                    par = like % 2
                    act.wait_ge(dn_ps, 2 * (s - 2) + 3)
                    if like >= 4:
                        act.wait_ge(y_st[par], 8 * (s - 2 - par))
                    act.copy(y[:, par, 0:512], ps[:, 4, :]).then_inc(y_ok, 1)
                    act.wait_ge(dn_ps, 2 * (s - 2) + 4)
                    act.copy(y[:, par, 512:D], ps[:, 5, :]).then_inc(y_ok, 1)
                    act.wait_ge(y_ok, 2 * (s - 2) + 2)
                    act.dma_start(y_dram[ds((s - 2) * P, P), :], y[:, par, :]).then_inc(y_st[par], 16)
            steps(act, step, NTILE + 2, 4, NTILE)
            for par in range(2):
                act.wait_ge(y_st[par], 16 * (NTILE // 2))

        @block.vector
        def _(dve):
            def step(j, like):
                dve.wait_ge(sg_ok, j + 1)
                if like >= 1:
                    dve.wait_ge(aT_ps, j)
                dve.tensor_tensor(a[:, :], sg[:, :], ps[:, 2 + like % 2, FE:2 * FE], ALU.mult).then_inc(a_ok, 1)
                dve.wait_ge(aT_ps, j + 1)
                if like >= 2:
                    dve.wait_ge(dn_ps, 2 * (j - 1) + 2)
                dve.tensor_copy(aT[like % 2][:, :, :], ps[:, 6, 0:FC * P].rearrange("p (c t) -> p c t", t=P)).then_inc(
                    aT_ok, 1)
            steps(dve, step, NTILE, 2, NTILE)

        @block.tensor
        def _(pe):
            def turn(j, like):
                pe.wait_ge(x_ld[like % 2], 8 * (j - like % 2) + 16)
                if like >= 1:
                    pe.wait_ge(xT_ok, j)
                for c in range(KC):
                    last = pe.transpose(ps[:, c // 4, c % 4 * P:(c % 4 + 1) * P], xg[:, like % 2, c * P:(c + 1) * P],
                                        ident[:, :])
                last.then_inc(tr_ps, 1)

            def gate_up(j, like):
                need = pe.value_load(TEXP[0:1, 0, ds(j, 1)], min_val=1, max_val=NE)
                off = pe.value_load(TEXP[0:1, 1, ds(j, 1)], min_val=0, max_val=(NBUF - 1) * ESZ)
                pe.wait_ge(xT_ok, j + 1)
                if like >= 2:
                    pe.wait_ge(a_ok, j - 1)
                pe.wait_ge(w_ok, need)
                for c in range(KC):
                    last = pe.matmul(ps[:, 2 + like % 2, :], xT[like % 2][:, c, :], W[:, ds(off + c * 2 * FE, 2 * FE)],
                                     start=(c == 0), stop=(c == KC - 1))
                last.then_inc(gu_ps, 1)

            def turn_a(j, like):
                pe.wait_ge(a_ok, j + 1)
                if like >= 1:
                    pe.wait_ge(aT_ok, j)
                for c in range(FC):
                    last = pe.transpose(ps[:, 6, c * P:(c + 1) * P], a[:, c * P:(c + 1) * P], ident[:, :])
                last.then_inc(aT_ps, 1)

            def down(j, like):
                off = pe.value_load(TEXP[0:1, 1, ds(j, 1)], min_val=0, max_val=(NBUF - 1) * ESZ)
                pe.wait_ge(aT_ok, j + 1)
                for h in range(2):
                    if like >= 1:
                        pe.wait_ge(y_ok, 2 * j - 1 + h)
                    for c in range(FC):
                        last = pe.matmul(ps[:, 4 + h, :], aT[like % 2][:, c, :],
                                         W[:, ds(off + (KC * 2 * FE + c * D + h * 512), 512)], start=(c == 0),
                                         stop=(c == FC - 1))
                    last.then_inc(dn_ps, 1)

            pe.sem_inc(dn_ps, 2)
            turn(0, 0)

            def step(s, like):
                if like < NTILE:
                    gate_up(s, like)
                if like + 1 < NTILE:
                    turn(s + 1, like + 1)
                if like >= 1:
                    down(s - 1, like - 1)
                if like < NTILE:
                    turn_a(s, like)
            steps(pe, step, NTILE + 1, 2, NTILE - 2)


def combine_block(nc, io, keep, y_dram):
    with ExitStack() as ctx:
        sem = Sems(nc, ctx, "c")
        sb = lambda n, s, d=F32: ctx.enter_context(nc.sbuf_tensor("c_" + n, s, d))
        X, POS, WT, nhalf = (keep[n] for n in ("x", "pos", "wt", "nhalf"))
        NBF = 3
        yg = sb("yg", [P, NBF, 2, D])
        o = sb("o", [P, NBF, D])
        gf = sb("gf", [P, D])
        junk = sb("junk", [P, D], BF16)
        st = sb("st", [P, 4 * NT])
        g_ld, y_ld, o_st = sem("g_ld"), sem("y_ld", 2 * NBF), sem("o_st", NBF)
        x0_ok, x_ok, sq_ok, mean_ok, r_ok, o_ok = (sem(n) for n in ("x0_ok", "x_ok", "sq_ok", "mean_ok", "r_ok", "o_ok"))
        block = ctx.enter_context(nc.Block())

        @block.sync
        def _(sp):
            sp.dma_start(gf[:, :], io["g_final"].to_broadcast([P, D])).then_inc(g_ld, 16)
            for t in range(NT):
                sp.wait_ge(o_ok, t + 1)
                if t < TS:
                    sp.dma_start(io["y_p"][t * P:(t + 1) * P, :], o[:, t % NBF, :]).then_inc(o_st[t % NBF], 16)
                else:
                    sp.dma_start(io["y_s"], o[0:ROWS_S, t % NBF, :]).then_inc(o_st[t % NBF], 16)
            for b in range(NBF):
                sp.wait_ge(o_st[b], 16 * len(range(b, NT, NBF)))

        @block.gpsimd
        def _(pool):
            def fetch(t):
                if t >= NBF:
                    pool.wait_ge(x_ok, t - NBF + 1)
                for k in range(2):
                    pool.indirect_dma_start(yg[:, t % NBF, k, :], None, y_dram[:, :],
                                            bass.IndirectOffsetOnAxis(ap=POS[:, k * NT + t:k * NT + t + 1], axis=0)
                                            ).then_inc(y_ld[2 * (t % NBF) + k], 16)
            fetch(0)
            fetch(1)
            for n in range(NT):
                if n + 2 < NT:
                    fetch(n + 2)
                pool.wait_ge(sq_ok, n + 1)
                pool.tensor_scalar(st[:, 4 * n + 1:4 * n + 2], st[:, 4 * n:4 * n + 1], 1.0 / D, EPS, ALU.mult,
                                   ALU.add).then_inc(mean_ok, 1)
                pool.wait_ge(mean_ok, n + 1)
                pool.tensor_tensor(st[:, 4 * n + 2:4 * n + 3], st[:, 4 * n + 1:4 * n + 2], nhalf[:, :],
                                   ALU.pow).then_inc(r_ok, 1)

        @block.scalar
        def _(act):
            for t in range(NT):
                act.wait_ge(x_ok, t + 1)
                if t:
                    act.wait_ge(sq_ok, t)
                act.activation(junk[:, :], X[:, t, :], ACT.Square, accum_out=st[:, 4 * t:4 * t + 1]).then_inc(sq_ok, 1)

        @block.vector
        def _(dve):
            def add(t):
                for k in range(2):
                    dve.wait_ge(y_ld[2 * (t % NBF) + k], 16 * (t // NBF + 1))
                    if k:
                        dve.wait_ge(x0_ok, t + 1)
                    dve.scalar_tensor_tensor(out=X[:, t, :], in0=yg[:, t % NBF, k, :], scalar=WT[:, k, t:t + 1],
                                             in1=X[:, t, :], op0=ALU.mult, op1=ALU.add).then_inc(x_ok if k else x0_ok, 1)
            add(0)
            dve.wait_ge(g_ld, 16)
            for t in range(NT):
                if t + 1 < NT:
                    add(t + 1)
                dve.wait_ge(r_ok, t + 1)
                if t >= NBF:
                    dve.wait_ge(o_st[t % NBF], 16 * (t // NBF))
                dve.scalar_tensor_tensor(out=o[:, t % NBF, :], in0=X[:, t, :], scalar=st[:, 4 * t + 2:4 * t + 3],
                                         in1=gf[:, :], op0=ALU.mult, op1=ALU.mult).then_inc(o_ok, 1)


def build(nc, io):
    x1_dram = nc.dram_tensor("x1_rows", [NT * P, D], F32, kind="Internal").ap()
    h_dram = nc.dram_tensor("h_rows", [NT * P, D], F32, kind="Internal").ap()
    y_dram = nc.dram_tensor("y_rows", [NTILE * P, D], F32, kind="Internal").ap()
    with ExitStack() as ctx:
        sb = lambda c, n, s, d=F32: c.enter_context(nc.sbuf_tensor(n, s, d))
        keep = {"nbuf": 4}
        keep["ps"] = ctx.enter_context(nc.psum_tensor("ps", [P, 8, 512], F32))
        keep["ident"] = sb(ctx, "ident", [P, P])
        keep["nhalf"] = sb(ctx, "nhalf", [P, 1])
        keep["gcol"] = sb(ctx, "gcol", [P, 4 * KC + NG])
        keep["win_ld"] = ctx.enter_context(nc.semaphore("win_ld"))
        keep["wkq_ld"] = ctx.enter_context(nc.semaphore("wkq_ld"))
        keep["pos"] = sb(ctx, "pos", [P, 2 * NT], I32)
        keep["wt"] = sb(ctx, "wt", [P, 2, NT])
        keep["idx"] = sb(ctx, "idx", [P, NTILE], I32)
        keep["texp"] = sb(ctx, "texp", [P, 2, NTILE], I32)
        keep["free"] = sb(ctx, "free", [P, NE], I32)
        with ExitStack() as att:
            keep["V"] = sb(att, "V", [P, MC, D])
            keep["KT"] = sb(att, "KT", [P, KC, NM])
            keep["wkq"] = sb(att, "wkq", [P, KC, D])
            with ExitStack() as mix:
                keep["w_in"] = sb(mix, "w_in", [P, KC, 3 * WA])
                memory_block(nc, io, keep)
                mixing_block(nc, io, keep, x1_dram)
            x_at = nc.sbuf_usable_end - NT * D * 4 - 64
            x_at -= x_at % 64
            keep["x"] = nc.alloc_sbuf_tensor_at("x", [P, NT, D], F32, offset=x_at)
            attention_block(nc, io, keep, x1_dram)
        routing_block(nc, io, keep, h_dram)
        experts_block(nc, io, keep, h_dram, y_dram)
        combine_block(nc, io, keep, y_dram)


def kernel(**inputs):
    import concourse.bacc as bacc
    from concourse.bass_utils import run_bass_kernel_spmd

    np_in = {k: np.asarray(v) for k, v in inputs.items()}
    nc = bacc.Bacc("TRN2", target_bir_lowering=False, num_devices=1)
    arrays, io = {}, {}

    def give(name, a):
        a = np.ascontiguousarray(a)
        arrays["in_" + name] = a
        io[name] = nc.dram_tensor("in_" + name, a.shape, mybir.dt.from_np(a.dtype), kind="ExternalInput").ap()

    def chunks(w):
        return w.reshape(w.shape[0] // P, P, w.shape[1]).transpose(1, 0, 2)

    f = np.float32
    x = np.zeros((NT * P, D), f)
    x[0:SEQ] = np_in["x_prompt"][0]
    x[SEQ:SEQ + ROWS_S] = np_in["x_sample"].reshape(ROWS_S, D)
    give("x", x)
    give("mem", np_in["mem_prompt"][0])
    gcol = np.concatenate([np_in[n].reshape(KC, P).T for n in ("g_mem", "g_mix", "g_xattn", "g_ffn")]
                          + [np_in["s_pool"].reshape(NG, P).T], axis=1)
    give("gcol", gcol)
    for n in ("w_xk", "w_xv", "w_xq", "w_xo", "w_in", "w_out"):
        give(n, chunks(np_in[n][0]))
    w_s = np_in["w_s"][0]
    give("wsT", w_s.transpose(2, 0, 1))
    wsTs = np.zeros((ROWS_S, HA, ROWS_S), f)
    for b in range(NB):
        wsTs[b * NL:(b + 1) * NL, :, b * NL:(b + 1) * NL] = w_s[:, 0:NL, 0:NL].transpose(2, 0, 1)
    give("wsTs", wsTs)
    band, bandp = banded()
    give("band", band.transpose(1, 0, 2, 3))
    give("bandp", bandp.transpose(1, 0, 2, 3))
    give("w_pool", np_in["w_pool"][0].transpose(1, 0, 2))
    give("g_v", np_in["g_v"])
    b_s = np_in["b_s"][0]
    give("bias", np.concatenate([b_s] + [b_s[:, 0:NL]] * NB, axis=1))
    give("head_of", np.repeat(np.eye(HA, dtype=f), DHA, axis=1))
    hist = np.zeros((P, WA), f)
    hist[0:NB * HIST] = np_in["state_pool"][0].reshape(NB * HIST, WA)
    give("hist", hist)
    give("state", np_in["state_pool"][0])
    kc = np_in["cache_mem_k"][0].reshape(NB, NM, XH, DC, P).transpose(0, 4, 2, 3, 1)
    give("kc", kc.reshape(NB, P, 2 * D))
    vc = np_in["cache_mem_v"][0].reshape(NB, MC, P, D).transpose(0, 2, 1, 3)
    give("vc", vc.reshape(NB, P, 2 * D))
    give("g_ffn", np_in["g_ffn"])
    give("g_final", np_in["g_final"].reshape(1, D))
    give("w_r", chunks(np.concatenate([np_in["w_group"][0], np_in["w_router"][0]], axis=1)))
    give("b_r", np.concatenate([np_in["b_group"], np_in["b_router"]], axis=1))
    give("before", np.triu(np.ones((P, P), f), 1))
    give("cst", np.concatenate([np.arange(4, 0, -1), P * np.arange(NT), np.arange(NTILE), np.arange(P)]).astype(f)[None])
    real = (np.arange(NT * P) < SEQ + ROWS_S).astype(f)
    give("tok", np.stack([(np.arange(NT * P) * real).reshape(NT, P).T, real.reshape(NT, P).T], axis=1).astype(f))
    gu = np.concatenate([np_in["w_gate"][0], np_in["w_up"][0]], axis=2).reshape(NE, KC, P, 2 * FE).transpose(0, 2, 1, 3)
    dn = np_in["w_down"][0].reshape(NE, FC, P, D).transpose(0, 2, 1, 3)
    give("w_e", np.concatenate([gu.reshape(NE * P, -1), dn.reshape(NE * P, -1)], axis=1))

    outs = [("y_p", (1, SEQ, D)), ("y_s", (NB, NL, D)), ("mem_k", (1, 1, NM, XH, XD)), ("mem_v", (1, 1, NM, XH, XD)),
            ("chunk_v_p", (1, 1, P, HA, DHA)), ("chunk_v_s", (1, NB, NL, HA, DHA)), ("pool_p", (1, 1, HIST, WA)),
            ("pool_s", (1, NB, HIST, WA))]
    views = {"y_p": "a s d -> (a s) d", "y_s": "b l d -> (b l) d", "mem_k": "a b m h d -> (a b m) (h d)",
             "mem_v": "a b m h d -> (a b m) (h d)", "chunk_v_p": "a b t h d -> (a b t) (h d)",
             "chunk_v_s": "a b t h d -> (a b t) (h d)", "pool_p": "a b t c -> (a b t) c", "pool_s": "a b t c -> (a b) t c"}
    for n, s in outs:
        io[n] = nc.dram_tensor("out_" + n, s, F32, kind="ExternalOutput").ap().rearrange(views[n])
    build(nc, io)
    r = run_bass_kernel_spmd(nc, [arrays], core_ids=[0])
    return tuple(r.results[0]["out_" + n] for n, _ in outs)
```

```python
from contextlib import ExitStack

import numpy as np
import concourse.bass as bass
from concourse import mybir

F32 = mybir.dt.float32
I32 = mybir.dt.int32
BF16 = mybir.dt.bfloat16
F32R = mybir.dt.float32r
ALU = mybir.AluOpType
ACT = mybir.ActivationFunctionType
AX_X = mybir.AxisListType.X
ds = bass.ds

P = 128
D = 1024
KC = D // P
SEQ = 1024
NB, NL = 8, 8
ROWS_S = NB * NL
NT = SEQ // P + 1
TS = NT - 1
WA = 512
HA, DHA = 8, 64
WINDOWS = (2, 4, 8, 16)
NG = len(WINDOWS)
HIST = max(WINDOWS) - 1
NM = 256
MC = NM // P
XH, XD = 4, 256
DC = XD // P
EG, EE = 4, 4
NE = EG * EE
FE = 256
FC = FE // P
EPS = 1e-6
PAIRS = 2 * (SEQ + ROWS_S)
NTILE = (PAIRS + NE * (P - 1)) // P
MIN_TILES = -(-PAIRS // P)
ESZ = KC * 2 * FE + FC * D
NL2 = EG + NE


def banded():
    main = np.zeros((3, P, NG, P), np.float32)
    prev = np.zeros((2, P, NG, P), np.float32)
    for g, w in enumerate(WINDOWS):
        for t in range(P):
            for k in range(w):
                if t - k >= 0:
                    main[0, t - k, g, t] = 1.0 / min(w, t + 1)
                    main[1, t - k, g, t] = 1.0 / w
                else:
                    prev[0, P + t - k, g, t] = 1.0 / w
            main[0, t, g, t] -= 1.0
            main[1, t, g, t] -= 1.0
        for b in range(NB):
            for l in range(NL):
                for k in range(w):
                    if l - k >= 0:
                        main[2, b * NL + l - k, g, b * NL + l] = 1.0 / w
                    else:
                        prev[1, b * HIST + HIST + l - k, g, b * NL + l] = 1.0 / w
                main[2, b * NL + l, g, b * NL + l] -= 1.0
    return main, prev


class Sems:
    def __init__(self, nc, ctx, tag):
        self.nc, self.ctx, self.tag = nc, ctx, tag

    def __call__(self, name, n=None):
        if n is None:
            return self.ctx.enter_context(self.nc.semaphore(f"{self.tag}_{name}"))
        return [self(f"{name}{i}") for i in range(n)]


def steps(eng, emit, count, lo, hi):
    for s in range(lo):
        emit(s, s)
    with eng.Fori(0, (hi - lo) // 2) as i:
        for u in range(2):
            emit(2 * i + (lo + u), lo + u)
    for s in range(hi, count):
        emit(s, s)


def bcast(ap, n):
    return ap.rearrange("p (a o) -> p a o", o=1).to_broadcast([ap.shape[0], ap.shape[1], n])


def memory_block(nc, io, keep):
    with ExitStack() as ctx:
        sem = Sems(nc, keep["all"], "m")
        sb = lambda n, s, d=F32: ctx.enter_context(nc.sbuf_tensor("m_" + n, s, d))
        wv = sb("wv", [P, KC, D])
        wk = keep["wkq"]
        xin = sb("xin", [P, MC, D])
        xs = sb("xs", [P, MC, D])
        hT = sb("hT", [P, MC, KC, P])
        knat = sb("knat", [P, MC, D])
        junk = sb("junk", [P, D], BF16)
        st = sb("st", [P, 4 * MC])
        ps, ident, nhalf = keep["ps"], keep["ident"], keep["nhalf"]
        x_ld, wk_ld, wv_ld, c_ld, win_ld = sem("x_ld", MC), sem("wk_ld", 2), sem("wv_ld"), sem("c_ld"), keep["win_ld"]
        id_ok, sq_ok, r_ok, xs_ok = sem("id_ok"), sem("sq_ok"), sem("r_ok"), sem("xs_ok")
        tr_ok, hT_ok, k_ps, v_ps, kn_ok, vn_ok = (sem(n) for n in ("tr_ok", "hT_ok", "k_ps", "v_ps", "kn_ok", "vn_ok"))
        kT_ps, kT_ok, out_st = sem("kT_ps"), sem("kT_ok"), sem("out_st")
        block = ctx.enter_context(nc.Block())

        @block.sync
        def _(sp):
            for m in range(MC):
                sp.dma_start(xin[:, m, :], io["mem"][m * P:(m + 1) * P, :]).then_inc(x_ld[m], 16)
            sp.dma_start(keep["gcol"][:, :], io["gcol"]).then_inc(c_ld, 16)
            for h in range(2):
                sp.dma_start(wk[:, :, h * 512:(h + 1) * 512], io["w_xk"][:, :, h * 512:(h + 1) * 512]).then_inc(wk_ld[h], 16)
            sp.dma_start(wv[:, :, :], io["w_xv"]).then_inc(wv_ld, 16)
            sp.dma_start(keep["w_in"][:, :, :], io["w_in"]).then_inc(win_ld, 16)
            load_mixing_buffers(sp, io, keep)
            for m in range(MC):
                sp.wait_ge(kn_ok, 3 + m)
                sp.dma_start(io["mem_k"][m * P:(m + 1) * P, :], knat[:, m, :]).then_inc(out_st, 16)
            for m in range(MC):
                sp.wait_ge(vn_ok, 2 * (m + 1))
                sp.dma_start(io["mem_v"][m * P:(m + 1) * P, :], keep["V"][:, m, :]).then_inc(out_st, 16)
            sp.wait_ge(out_st, 16 * 2 * MC)

        @block.gpsimd
        def _(pool):
            pool.memset(ident[:, :], 0.0).then_inc(id_ok, 1)
            pool.memset(nhalf[:, :], -0.5).then_inc(id_ok, 1)
            pool.wait_ge(id_ok, 2)
            pool.affine_select(out=ident[:, :], in_=ident[:, :], compare_op=ALU.not_equal, fill=1.0, base=0,
                               pattern=[[-1, P]], channel_multiplier=1).then_inc(id_ok, 1)
            for m in range(MC):
                pool.wait_ge(sq_ok, m + 1)
                pool.tensor_scalar(st[:, 4 * m + 1:4 * m + 2], st[:, 4 * m:4 * m + 1], 1.0 / D, EPS, ALU.mult,
                                   ALU.add).then_inc(r_ok, 1)
                pool.wait_ge(r_ok, 2 * m + 1)
                pool.tensor_tensor(st[:, 4 * m + 2:4 * m + 3], st[:, 4 * m + 1:4 * m + 2], nhalf[:, :],
                                   ALU.pow).then_inc(r_ok, 1)

        @block.scalar
        def _(act):
            for m in range(MC):
                act.wait_ge(x_ld[m], 16)
                if m:
                    act.wait_ge(sq_ok, m)
                act.activation(junk[:, :], xin[:, m, :], ACT.Square, accum_out=st[:, 4 * m:4 * m + 1]).then_inc(sq_ok, 1)
            for h in range(2):
                for m in range(MC):
                    act.wait_ge(k_ps, MC * h + m + 1)
                    act.copy(knat[:, m, h * 512:(h + 1) * 512], ps[:, 2 + 2 * m + h, :]).then_inc(kn_ok, 1)
            for m in range(MC):
                for h in range(2):
                    act.wait_ge(v_ps, 2 * m + h + 1)
                    bank = (6, 7, 2, 3)[2 * m + h]
                    act.copy(keep["V"][:, m, h * 512:(h + 1) * 512], ps[:, bank, :]).then_inc(vn_ok, 1)

        @block.vector
        def _(dve):
            dve.wait_ge(c_ld, 16)
            for m in range(MC):
                dve.wait_ge(r_ok, 2 * m + 2)
                dve.tensor_scalar(xs[:, m, :], xin[:, m, :], st[:, 4 * m + 2:4 * m + 3], None, ALU.mult).then_inc(xs_ok, 1)
            for m in range(MC):
                dve.wait_ge(tr_ok, m + 1)
                dve.tensor_tensor(hT[:, m, :, :], ps[:, 0:2, :].rearrange("p b (c t) -> p (b c) t", t=P),
                                  bcast(keep["gcol"][:, 0:KC], P), ALU.mult).then_inc(hT_ok, 1)
            for m in range(MC):
                dve.wait_ge(kT_ps, m + 1)
                dve.tensor_copy(keep["KT"][:, :, m * P:(m + 1) * P],
                                ps[:, 4:6, :].rearrange("p b (c t) -> p (b c) t", t=P)).then_inc(kT_ok, 1)

        @block.tensor
        def _(pe):
            pe.wait_ge(id_ok, 3)
            for m in range(MC):
                pe.wait_ge(xs_ok, m + 1)
                if m:
                    pe.wait_ge(hT_ok, m)
                for c in range(KC):
                    last = pe.transpose(ps[:, c // 4, c % 4 * P:(c % 4 + 1) * P], xs[:, m, c * P:(c + 1) * P], ident[:, :])
                last.then_inc(tr_ok, 1)

            def project(w, m, h, bank):
                pe.wait_ge(hT_ok, m + 1)
                for c in range(KC):
                    last = pe.matmul(ps[:, bank, :], hT[:, m, c, :], w[:, c, h * 512:(h + 1) * 512],
                                     start=(c == 0), stop=(c == KC - 1))
                return last

            for h in range(2):
                pe.wait_ge(wk_ld[h], 16)
                for m in range(MC):
                    project(wk, m, h, 2 + 2 * m + h).then_inc(k_ps, 1)
            pe.wait_ge(wv_ld, 16)
            for m in range(MC):
                if m:
                    pe.wait_ge(kn_ok, 3)
                for h in range(2):
                    project(wv, m, h, (6, 7, 2, 3)[2 * m + h]).then_inc(v_ps, 1)
            pe.wait_ge(kn_ok, 4)
            for m in range(MC):
                if m:
                    pe.wait_ge(kT_ok, m)
                for c in range(KC):
                    last = pe.transpose(ps[:, 4 + c // 4, c % 4 * P:(c % 4 + 1) * P], knat[:, m, c * P:(c + 1) * P],
                                        ident[:, :])
                last.then_inc(kT_ps, 1)


def mixing_buffers(nc, ctx, io, keep):
    sb = lambda n, s: keep.update({n: ctx.enter_context(nc.sbuf_tensor("a_" + n, s, F32))})
    sb("wsT", [P, HA, P])
    sb("wsTs", [ROWS_S, HA, ROWS_S])
    sb("band", [P, 3, NG, P])
    sb("bandp", [P, 2, NG, P])
    sb("w_pool", [P, NG, P])
    sb("gv", [P, WA])
    sb("bias", [HA, P + ROWS_S])
    sb("head_of", [HA, WA])
    sb("hist", [P, WA])
    sb("xin", [P, 2, D])
    sem = Sems(nc, keep["all"], "a")
    keep["x_ld"], keep["mix_ld"] = sem("x_ld", 2), sem("mix_ld")


def load_mixing_buffers(sp, io, keep):
    for t in range(2):
        sp.dma_start(keep["xin"][:, t, :], io["x"][t * P:(t + 1) * P, :]).then_inc(keep["x_ld"][t], 16)
    consts = [(keep["wsT"][:, :, :], io["wsT"]), (keep["wsTs"][:, :, :], io["wsTs"]),
              (keep["band"][:, :, :, :], io["band"]), (keep["bandp"][:, :, :, :], io["bandp"]),
              (keep["w_pool"][:, :, :], io["w_pool"]), (keep["gv"][:, :], io["g_v"].to_broadcast([P, WA])),
              (keep["bias"][:, :], io["bias"]), (keep["head_of"][:, :], io["head_of"]), (keep["hist"][:, :], io["hist"])]
    for dst, src in consts:
        sp.dma_start(dst, src).then_inc(keep["mix_ld"], 16)
    keep["mix_loads"] = len(consts)


def mixing_block(nc, io, keep, x1_dram):
    with ExitStack() as ctx:
        sem = Sems(nc, keep["all"], "a")
        sb = lambda n, s, d=F32: ctx.enter_context(nc.sbuf_tensor("a_" + n, s, d))
        w_in, ps, ident, nhalf = keep["w_in"], keep["ps"], keep["ident"], keep["nhalf"]
        w_out = sb("w_out", [P, KC, D])
        (wsT, wsTs, band, bandp, w_pool, gv, bias, head_of, hist, xin, x_ld, mix_ld) = (
            keep[n] for n in ("wsT", "wsTs", "band", "bandp", "w_pool", "gv", "bias", "head_of", "hist", "xin", "x_ld",
                              "mix_ld"))
        xr = sb("xr", [P, 2, D])
        xs = sb("xs", [P, 2, D])
        hT = [sb(f"hT{i}", [P, KC, P]) for i in range(2)]
        z = [sb(f"z{i}", [P, WA]) for i in range(2)]
        u, vg, vn, a, poolT = (sb(n, [P, WA]) for n in ("u", "vg", "vn", "a", "poolT"))
        catT = sb("catT", [P, KC, P])
        junk, junkv = sb("junk", [P, D], BF16), sb("junkv", [P, WA], BF16)
        st = sb("st", [P, 16])
        gmix, spool = keep["gcol"][:, KC:2 * KC], keep["gcol"][:, 4 * KC:4 * KC + NG]
        win_ld = keep["win_ld"]
        wout_ld, xr_ld, x1_st = sem("wout_ld"), sem("xr_ld", 2), sem("x1_st", 2)
        (mask_ok, sq_ok, mean_ok, r_ok, xs_ok, tr_ps, hT_ok, v_ps, z_ps, u_ps, vg_ok, vsq_ok, vmean_ok, vr_ok, vn_ok, z_ok,
         u_ok, pool_ps, mix_ps, poolT_ok, a_ok, y_ps, aT_ps, y_ok, aT_ok, out_ps, x1_ok, out_st) = (
            sem(n) for n in ("mask_ok", "sq_ok", "mean_ok", "r_ok", "xs_ok", "tr_ps", "hT_ok", "v_ps", "z_ps", "u_ps",
                             "vg_ok", "vsq_ok", "vmean_ok", "vr_ok", "vn_ok", "z_ok", "u_ok", "pool_ps", "mix_ps",
                             "poolT_ok", "a_ok", "y_ps", "aT_ps", "y_ok", "aT_ok", "out_ps", "x1_ok", "out_st"))
        wkq_ld, state_st = keep["wkq_ld"], sem("state_st")
        block = ctx.enter_context(nc.Block())

        @block.sync
        def _(sp):
            def load_x(t, like):
                if like >= 2:
                    sp.wait_ge(xs_ok, t - 1)
                sp.dma_start(xin[:, like % 2, :], io["x"][ds(t * P, P), :]).then_inc(x_ld[like % 2], 16)

            def load_xr(t, like):
                if like >= 2:
                    sp.wait_ge(x1_st[like % 2], 8 * (t - like % 2))
                sp.dma_start(xr[:, like % 2, :], io["x"][ds(t * P, P), :]).then_inc(xr_ld[like % 2], 16)

            sp.dma_start(w_out[:, :, :], io["w_out"]).then_inc(wout_ld, 16)
            load_xr(0, 0)
            sp.dma_start(keep["wkq"][:, :, :], io["w_xq"]).then_inc(wkq_ld, 16)
            sp.dma_start(io["pool_s"][:, 0:HIST - NL, :], io["state"][:, NL:HIST, :]).then_inc(state_st, 16)

            def step(s, like):
                if like + 2 < NT:
                    load_x(s + 2, like + 2)
                if like >= 1:
                    sp.wait_ge(x1_ok, 2 * s)
                    sp.dma_start(x1_dram[ds((s - 1) * P, P), :], xr[:, (like - 1) % 2, :]).then_inc(x1_st[(like - 1) % 2], 16)
                if like + 1 < NT:
                    load_xr(s + 1, like + 1)
            steps(sp, step, NT + 1, 2, 6)
            sp.wait_ge(x1_st[0], 16 * 5)
            sp.wait_ge(x1_st[1], 16 * 4)
            sp.wait_ge(out_st, 16 * 4)
            sp.wait_ge(state_st, 16)

        @block.gpsimd
        def _(pool):
            pool.wait_ge(mix_ld, 16 * keep["mix_loads"])
            pool.affine_select(out=wsT[:, :, :], in_=wsT[:, :, :], compare_op=ALU.is_ge, fill=0.0, base=0,
                               pattern=[[0, HA], [1, P]], channel_multiplier=-1).then_inc(mask_ok, 1)
            pool.affine_select(out=wsTs[:, :, :], in_=wsTs[:, :, :], compare_op=ALU.is_ge, fill=0.0, base=0,
                               pattern=[[0, HA], [1, ROWS_S]], channel_multiplier=-1).then_inc(mask_ok, 1)

            def x_rms(t, like):
                c = 4 * (like % 2)
                pool.wait_ge(sq_ok, t + 1)
                pool.tensor_scalar(st[:, c + 1:c + 2], st[:, c:c + 1], 1.0 / D, EPS, ALU.mult, ALU.add).then_inc(mean_ok, 1)
                pool.wait_ge(mean_ok, t + 1)
                if like >= 2:
                    pool.wait_ge(xs_ok, t - 1)
                pool.tensor_tensor(st[:, c + 2:c + 3], st[:, c + 1:c + 2], nhalf[:, :], ALU.pow).then_inc(r_ok, 1)

            x_rms(0, 0)
            x_rms(1, 1)

            def step(s, like):
                if like + 2 < NT:
                    x_rms(s + 2, like + 2)
                if like < NT:
                    pool.wait_ge(vsq_ok, s + 1)
                    pool.tensor_scalar(st[:, 9:10], st[:, 8:9], 1.0 / WA, EPS, ALU.mult, ALU.add).then_inc(vmean_ok, 1)
                    pool.wait_ge(vmean_ok, s + 1)
                    if like >= 1:
                        pool.wait_ge(vn_ok, s)
                    pool.tensor_tensor(st[:, 10:11], st[:, 9:10], nhalf[:, :], ALU.pow).then_inc(vr_ok, 1)
                if like == TS - 1:
                    pool.wait_ge(vn_ok, s + 1)
                    pool.dma_start(io["chunk_v_p"], vn[:, :]).then_inc(out_st, 16)
                    pool.wait_ge(z_ok, s + 1)
                    pool.dma_start(io["pool_p"], z[(TS - 1) % 2][P - HIST:P, :]).then_inc(out_st, 16)
                if like == TS:
                    pool.wait_ge(vn_ok, s + 1)
                    pool.dma_start(io["chunk_v_s"], vn[0:ROWS_S, :]).then_inc(out_st, 16)
                    pool.wait_ge(z_ok, s + 1)
                    pool.dma_start(io["pool_s"][:, HIST - NL:HIST, :], z[TS % 2][0:ROWS_S, :]).then_inc(out_st, 16)
            for s in range(NT):
                step(s, s)

        @block.scalar
        def _(act):
            def square(t, like):
                act.wait_ge(x_ld[like % 2], 8 * (t - like % 2) + 16)
                if like >= 1:
                    act.wait_ge(sq_ok, t)
                if like >= 2:
                    act.wait_ge(mean_ok, t - 1)
                act.activation(junk[:, :], xin[:, like % 2, :], ACT.Square,
                               accum_out=st[:, 4 * (like % 2):4 * (like % 2) + 1]).then_inc(sq_ok, 1)

            square(0, 0)
            square(1, 1)

            def step(s, like):
                if like >= 1:
                    act.wait_ge(pool_ps, s)
                    if like >= 2:
                        act.wait_ge(y_ps, s - 1)
                    act.copy(poolT[:, :], ps[:, 6, :]).then_inc(poolT_ok, 1)
                if like + 2 < NT:
                    square(s + 2, like + 2)
                if like < NT:
                    act.wait_ge(v_ps, s + 1)
                    if like >= 1:
                        act.wait_ge(vn_ok, s)
                    act.activation(vg[:, :], ps[:, 3, :], ACT.Gelu_apprx_tanh).then_inc(vg_ok, 1)
                    act.wait_ge(vg_ok, s + 1)
                    if like >= 1:
                        act.wait_ge(vmean_ok, s)
                    act.activation(junkv[:, :], vg[:, :], ACT.Square, accum_out=st[:, 8:9]).then_inc(vsq_ok, 1)
                if like >= 1:
                    act.wait_ge(aT_ps, s)
                    if like >= 2:
                        act.wait_ge(out_ps, 2 * s - 2)
                    act.copy(catT[:, 0:KC // 2, :], ps[:, 5, :].rearrange("p (c t) -> p c t", t=P)).then_inc(aT_ok, 1)
                if like < NT:
                    act.wait_ge(u_ps, s + 1)
                    if like >= 1:
                        act.wait_ge(a_ok, s)
                    act.activation(u[:, :], ps[:, 2, :], ACT.Gelu_apprx_tanh).then_inc(u_ok, 1)
            steps(act, step, NT + 1, 2, 6)

        @block.vector
        def _(dve):
            def scale(t, like):
                dve.wait_ge(r_ok, t + 1)
                if like >= 2:
                    dve.wait_ge(tr_ps, t - 1)
                dve.tensor_scalar(xs[:, like % 2, :], xin[:, like % 2, :], st[:, 4 * (like % 2) + 2:4 * (like % 2) + 3], None,
                                  ALU.mult).then_inc(xs_ok, 1)

            def read_hT(t, like):
                dve.wait_ge(tr_ps, t + 1)
                if like >= 2:
                    dve.wait_ge(u_ps, t - 1)
                dve.tensor_tensor(hT[like % 2][:, :, :], ps[:, 0:2, :].rearrange("p b (c t) -> p (b c) t", t=P),
                                  bcast(gmix, P), ALU.mult).then_inc(hT_ok, 1)

            scale(0, 0)
            scale(1, 1)
            read_hT(0, 0)

            def step(s, like):
                if like >= 1:
                    dve.wait_ge(mix_ps, s)
                    dve.wait_ge(u_ok, s)
                    if like >= 2:
                        dve.wait_ge(aT_ps, s - 1)
                    dve.tensor_tensor(a[:, :], u[:, :], ps[:, 5, :], ALU.mult).then_inc(a_ok, 1)
                if like + 2 < NT:
                    scale(s + 2, like + 2)
                if like + 1 < NT:
                    read_hT(s + 1, like + 1)
                if like >= 1:
                    dve.wait_ge(y_ps, s)
                    if like >= 2:
                        dve.wait_ge(out_ps, 2 * s - 2)
                    dve.tensor_tensor(catT[:, KC // 2:KC, :], ps[:, 6, :].rearrange("p (c t) -> p c t", t=P),
                                      bcast(spool, P), ALU.mult).then_inc(y_ok, 1)
                if like < NT:
                    if like == TS:
                        dve.wait_ge(out_st, 16 * 2)
                    dve.wait_ge(vr_ok, s + 1)
                    if like >= 1:
                        dve.wait_ge(mix_ps, s)
                    dve.scalar_tensor_tensor(out=vn[:, :], in0=vg[:, :], scalar=st[:, 10:11], in1=gv[:, :],
                                             op0=ALU.mult, op1=ALU.mult).then_inc(vn_ok, 1)
                    dve.wait_ge(z_ps, s + 1)
                    if like >= 2:
                        dve.wait_ge(pool_ps, s)
                    dve.tensor_copy(z[like % 2][:, :], ps[:, 4, :]).then_inc(z_ok, 1)
                if like >= 1:
                    if like == 1:
                        dve.wait_ge(xr_ld[0], 16)
                    else:
                        par = (like - 1) % 2
                        dve.wait_ge(xr_ld[par], 8 * (s - 1 - par) + 16)
                    for h in range(2):
                        dve.wait_ge(out_ps, 2 * s - 1 + h)
                        half = xr[:, (like - 1) % 2, h * 512:(h + 1) * 512]
                        dve.tensor_tensor(half, half, ps[:, 7 if h == 0 else 5, :], ALU.add).then_inc(x1_ok, 1)
            dve.wait_ge(mix_ld, 16 * keep["mix_loads"])
            steps(dve, step, NT + 1, 2, 6)

        @block.tensor
        def _(pe):
            def turn(t, like):
                pe.wait_ge(xs_ok, t + 1)
                if like >= 1:
                    pe.wait_ge(hT_ok, t)
                for c in range(KC):
                    last = pe.transpose(ps[:, c // 4, c % 4 * P:(c % 4 + 1) * P], xs[:, like % 2, c * P:(c + 1) * P],
                                        ident[:, :])
                last.then_inc(tr_ps, 1)

            def project(s, like, bank, col, done):
                for c in range(KC):
                    last = pe.matmul(ps[:, bank, :], hT[like % 2][:, c, :], w_in[:, c, col:col + WA],
                                     start=(c == 0), stop=(c == KC - 1))
                last.then_inc(done, 1)

            def mix(t, like):
                pe.wait_ge(z_ok, t + 1)
                if like >= 1:
                    pe.wait_ge(y_ok, t)
                var = 0 if like == 0 else 2 if like == TS else 1
                before = None if like == 0 else hist if like == TS else z[(like - 1) % 2]
                for g in range(NG):
                    cols = slice(g * P, (g + 1) * P)
                    last = pe.matmul(ps[:, 6, cols], z[like % 2][:, cols], band[:, var, g, :], start=True,
                                     stop=before is None)
                    if before is not None:
                        last = pe.matmul(ps[:, 6, cols], before[:, cols], bandp[:, 0 if like < TS else 1, g, :],
                                         start=False, stop=True)
                last.then_inc(pool_ps, 1)
                pe.wait_ge(vn_ok, t + 1)
                if like >= 1:
                    pe.wait_ge(x1_ok, 2 * t)
                rows = P if like < TS else ROWS_S
                wt, b0 = (wsT, 0) if like < TS else (wsTs, P)
                pe.matmul(ps[0:rows, 5, :], bias[:, b0:b0 + rows], head_of[:, :], start=True, stop=False,
                          skip_group_check=True)
                for h in range(HA):
                    last = pe.matmul(ps[0:rows, 5, h * DHA:(h + 1) * DHA], wt[0:rows, h, 0:rows],
                                     vn[0:rows, h * DHA:(h + 1) * DHA], start=False, stop=(h == HA - 1),
                                     skip_group_check=True)
                last.then_inc(mix_ps, 1)

            def turn_mixed(t, like):
                pe.wait_ge(poolT_ok, t + 1)
                for g in range(NG):
                    last = pe.matmul(ps[:, 6, g * P:(g + 1) * P], w_pool[:, g, :], poolT[:, g * P:(g + 1) * P],
                                     start=True, stop=True)
                last.then_inc(y_ps, 1)
                pe.wait_ge(a_ok, t + 1)
                for c in range(WA // P):
                    last = pe.transpose(ps[:, 5, c * P:(c + 1) * P], a[:, c * P:(c + 1) * P], ident[:, :])
                last.then_inc(aT_ps, 1)

            def out(t, like):
                pe.wait_ge(aT_ok, t + 1)
                pe.wait_ge(y_ok, t + 1)
                for h in range(2):
                    if h == 0 and like >= 1:
                        pe.wait_ge(x1_ok, 2 * t)
                    for c in range(KC):
                        last = pe.matmul(ps[:, 7 if h == 0 else 5, :], catT[:, c, :], w_out[:, c, h * 512:(h + 1) * 512],
                                         start=(c == 0), stop=(c == KC - 1))
                    last.then_inc(out_ps, 1)

            turn(0, 0)
            pe.wait_ge(mix_ld, 16 * keep["mix_loads"])
            pe.wait_ge(mask_ok, 2)
            pe.wait_ge(win_ld, 16)

            def step(s, like):
                if like >= 1:
                    mix(s - 1, like - 1)
                if like + 1 < NT:
                    turn(s + 1, like + 1)
                if like < NT:
                    pe.wait_ge(hT_ok, s + 1)
                    if like >= 1:
                        pe.wait_ge(vg_ok, s)
                    project(s, like, 3, WA, v_ps)
                if like >= 1:
                    turn_mixed(s - 1, like - 1)
                if like < NT:
                    if like >= 1:
                        pe.wait_ge(z_ok, s)
                    project(s, like, 4, 2 * WA, z_ps)
                    if like >= 1:
                        pe.wait_ge(u_ok, s)
                    project(s, like, 2, 0, u_ps)
                if like >= 1:
                    if like == 1:
                        pe.wait_ge(wout_ld, 16)
                    out(s - 1, like - 1)
            steps(pe, step, NT + 1, 2, 6)


def attention_plan():
    pairs = TS // 2
    plan = [("th", 0), ("qs", 0), ("th", 1), ("qs", 1), ("qst",), ("th", 2)]
    spread = {1: 3, 2: 3, 3: 2}
    v = iter(range(NB, 2 * NB))
    for s in range(pairs + 1):
        items = [("kv", next(v)) for _ in range(spread.get(s, 0))]
        if s == 0:
            for c in range(KC // 2):
                plan += [("kv", 2 * c), ("kv", 2 * c + 1)] + [("ts",)] * (c == KC // 2 - 1) + [("q", 0, c)]
            plan += [("th", 3), ("sc", 0, 0), ("tps",), ("th", 4), ("sc", 0, 1)]
            continue
        else:
            if s == 1:
                plan += items[0:2] + [("tp", 0, 0)] + items[2:3] + [("tp", 0, 1)]
                items = []
            else:
                plan += [("tp", s - 1, 0)] + items[0:1] + [("tp", s - 1, 1)] + items[1:2]
            plan += [("oT", s - 1, c) for c in range(KC // 2)]
            if s < pairs:
                plan += [("q", s, c) for c in range(KC // 2)]
        outs = [("out", s - 1, j, h) for j in range(2) for h in range(2)] if s else []
        if s < pairs:
            plan += [("sc", s, 0), ("sc", s, 1)] + items[2:3]
            if s + 1 < pairs:
                plan += [("th", 2 * s + 3)] + outs[0:1] + [("th", 2 * s + 4)] + outs[1:]
                continue
        plan += outs
    plan += [("outs", 0), ("outs", 1)]
    ops, seen, rot = [], {}, 0
    for op in plan:
        kind = op[0]
        seen[kind] = seen.get(kind, 0) + 1
        bank = None
        if kind not in ("th", "tp", "sc", "ts") and not (kind == "kv" and op[1] < NB):
            bank, rot = rot, rot + 1
        ops.append((op, seen[kind], bank))
    return ops


def attention_block(nc, io, keep, x1_dram, y_dram):
    plan = attention_plan()
    PAIR = 2 * P
    SCALE = float(XD) ** -0.5
    with ExitStack() as ctx:
        sem = Sems(nc, keep["all"], "t")
        sb = lambda n, s, d=F32: ctx.enter_context(nc.sbuf_tensor("t_" + n, s, d))
        w_q, KT, V, X, ps, ident, nhalf = (keep[n] for n in ("wkq", "KT", "V", "x", "ps", "ident", "nhalf"))
        w_o = sb("w_o", [P, KC, D])
        hT, qT = (sb(n, [P, KC, PAIR]) for n in ("hT", "qT"))
        shared = sb("shared", [P, 2 * KC, PAIR])
        pT, oT = shared[:, 0:KC, :], shared[:, KC:2 * KC, :]
        E = sb("E", [P, 2, D])
        ring = sb("ring", [P, 3, 2 * D])
        xs = sb("xs", [P, D])
        junk = sb("junk", [P, D], BF16)
        oS = sb("oS", [P, KC, ROWS_S])
        qSm = shared[:, :, :].rearrange("p k n -> p (k n)").rearrange("p (c b r) -> p c b r", c=KC, r=ROWS_S)
        ES, pS = sb("ES", [ROWS_S, D]), sb("pS", [P, XH * MC, ROWS_S])
        st = sb("st", [P, 4 * NT])
        sm = sb("sm", [P, 3, 4 * XH])
        gx = keep["gcol"][:, 2 * KC:3 * KC]
        NRING = 3
        xS_ld, x_ld, wo_ld, kv_ld, fill_st = sem("xS_ld"), sem("x_ld"), sem("wo_ld"), sem("kv_ld", NRING), sem("fill_st")
        sq_ok, r_ok, xs_ok = (sem(n) for n in ("sq_ok", "r_ok", "xs_ok"))
        done = {k: sem(k + "_ps") for k in ("th", "qs", "qst", "kv", "tps", "tp", "oT", "q", "sc", "out", "outs")}
        t_ok, rot_ok = sem("t_ok"), sem("rot_ok", 2)
        zero_ok, ES_ok = sem("zero_ok"), sem("ES_ok")
        max_ok, nb_ok, exp_ok, inv_ok, p_ok = (sem(n) for n in ("max_ok", "nb_ok", "exp_ok", "inv_ok", "p_ok"))
        SOFT = {}
        TPOS = {}
        for op, _, _ in plan:
            if op[0] in ("sc", "ts"):
                SOFT[op] = len(SOFT)
            if op[0] in ("th", "tp"):
                TPOS[op] = len(TPOS)
        tile_of = lambda n: TS if n == 0 else n - 1

        def read_out(eng, which):
            for b in (0, 1):
                uses = [rot for op, _, rot in plan if rot is not None and rot % 2 == b and which(op)]
                if uses:
                    eng.wait_ge(rot_ok[b], max(uses) // 2 + 1)

        block = ctx.enter_context(nc.Block())

        @block.sync
        def _(sp):
            def load_kv(i):
                if i >= NRING:
                    sp.wait_ge(done["kv"], i - NRING + 1)
                src = io["kc"][i] if i < NB else io["vc"][i - NB]
                sp.dma_start(ring[:, i % NRING, :], src).then_inc(kv_ld[i % NRING], 16)
            sp.dma_start(X[:, TS, :], x1_dram[TS * P:NT * P, :]).then_inc(xS_ld, 16)
            for t in range(TS):
                sp.dma_start(X[:, t, :], x1_dram[t * P:(t + 1) * P, :]).then_inc(x_ld, 16)
            for i in range(NB):
                load_kv(i)
            sp.dma_start(w_o[:, :, :], io["w_xo"]).then_inc(wo_ld, 16)
            for i in range(NB, 2 * NB):
                load_kv(i)
            load_routing_buffers(sp, io, keep)
            for lo in range(MIN_TILES, NTILE, NT):
                n = min(NT, NTILE - lo) * P
                sp.dma_start(y_dram[lo * P:lo * P + n, :], io["x"][0:n, :]).then_inc(fill_st, 16)
            sp.wait_ge(fill_st, 16 * -(-(NTILE - MIN_TILES) // NT))

        @block.gpsimd
        def _(pool):
            pool.memset(qSm[:, :, :, :], 0.0).then_inc(zero_ok, 1)
            for n in range(NT):
                pool.wait_ge(sq_ok, n + 1)
                pool.tensor_scalar(st[:, 4 * n + 1:4 * n + 2], st[:, 4 * n:4 * n + 1], 1.0 / D, EPS, ALU.mult,
                                   ALU.add).then_inc(r_ok, 1)
                pool.wait_ge(r_ok, 2 * n + 1)
                pool.tensor_tensor(st[:, 4 * n + 2:4 * n + 3], st[:, 4 * n + 1:4 * n + 2], nhalf[:, :],
                                   ALU.pow).then_inc(r_ok, 1)

        @block.scalar
        def _(act):
            def square(n):
                act.wait_ge(xS_ld if n == 0 else x_ld, 16 if n == 0 else 16 * TS)
                if n:
                    act.wait_ge(sq_ok, n)
                act.activation(junk[:, :], X[:, tile_of(n), :], ACT.Square,
                               accum_out=st[:, 4 * n:4 * n + 1]).then_inc(sq_ok, 1)

            def exps(k, cols, out, groups):
                act.wait_ge(nb_ok, k + 1)
                rows = out.shape[0]
                for g in range(groups):
                    last = act.activation(out[:, g * NM:(g + 1) * NM], cols[:, g * NM:(g + 1) * NM], ACT.Exp,
                                          bias=sm[0:rows, 1, 4 * (k % 4) + g:4 * (k % 4) + g + 1], scale=SCALE,
                                          accum_out=sm[0:rows, 2, 4 * (k % 4) + g:4 * (k % 4) + g + 1])
                return last

            square(0)
            square(1)
            for op, n, rot in plan:
                kind = op[0]
                bank = None if rot is None else ps[:, 2 + rot % 2, :]
                if kind == "th" and op[1] + 2 < NT:
                    square(op[1] + 2)
                elif kind == "qs":
                    act.wait_ge(done["qs"], n)
                    act.copy(E[0:ROWS_S, 0, op[1] * 512:(op[1] + 1) * 512], bank[0:ROWS_S, :]).then_inc(rot_ok[rot % 2], 1)
                elif kind == "qst":
                    act.wait_ge(done["qst"], 1)
                    act.wait_ge(zero_ok, 1)
                    for b in range(NB):
                        own = slice(b * NL, (b + 1) * NL)
                        last = act.copy(qSm[:, :, b, own], bank.rearrange("p (c t) -> p c t", t=ROWS_S)[:, :, own])
                    last.then_inc(rot_ok[rot % 2], 1)
                elif kind == "q":
                    act.wait_ge(done["q"], n)
                    if op[1]:
                        act.wait_ge(done["sc"], 2 * op[1])
                    act.copy(qT[:, 2 * op[2]:2 * op[2] + 2, :], bank.rearrange("p (c t) -> p c t", t=PAIR)).then_inc(
                        rot_ok[rot % 2], 1)
                elif kind == "kv" and op[1] >= NB:
                    act.wait_ge(done["kv"], n)
                    b = op[1] - NB
                    act.copy(oS[:, :, b * NL:(b + 1) * NL], bank[:, 0:64].rearrange("p (c r) -> p c r", r=NL)).then_inc(
                        rot_ok[rot % 2], 1)
                elif kind == "sc":
                    if op[1]:
                        act.wait_ge(done["tp"], 2 * op[1] - 1 + op[2])
                    j = op[2]
                    exps(SOFT[op], ps[:, 4 + 2 * j:6 + 2 * j, :].rearrange("p b n -> p (b n)"), E[:, j, :], XH).then_inc(
                        exp_ok, 1)
                elif kind == "ts":
                    exps(SOFT[op], ps[0:ROWS_S, 6:8, :].rearrange("p b n -> p (b n)"), ES[:, :], XH).then_inc(exp_ok, 1)
                elif kind == "tps":
                    act.wait_ge(done["tps"], 1)
                    act.copy(pS[:, :, :], bank.rearrange("p (i r) -> p i r", r=ROWS_S)).then_inc(rot_ok[rot % 2], 1)

        @block.vector
        def _(dve):
            def scale(n):
                dve.wait_ge(r_ok, 2 * n + 2)
                if n:
                    dve.wait_ge(done["th"], n)
                dve.tensor_scalar(xs[:, :], X[:, tile_of(n), :], st[:, 4 * n + 2:4 * n + 3], None, ALU.mult).then_inc(xs_ok, 1)

            def softmax(k, scores, out, groups, wait, ok):
                dve.wait_ge(*wait)
                c, rows = 4 * (k % 4), out.shape[0]
                dve.tensor_reduce(sm[0:rows, 0, c:c + groups], scores, AX_X, ALU.max).then_inc(max_ok, 1)
                dve.wait_ge(max_ok, k + 1)
                dve.tensor_scalar(sm[0:rows, 1, c:c + groups], sm[0:rows, 0, c:c + groups], -SCALE, None, ALU.mult).then_inc(nb_ok, 1)
                dve.wait_ge(exp_ok, k + 1)
                dve.reciprocal(sm[0:rows, 0, c:c + groups], sm[0:rows, 2, c:c + groups]).then_inc(inv_ok, 1)
                dve.wait_ge(inv_ok, k + 1)
                return dve.tensor_tensor(out, out, bcast(sm[0:rows, 0, c:c + groups], NM), ALU.mult).then_inc(ok, 1)

            scale(0)
            for op, n, rot in plan:
                kind = op[0]
                bank = None if rot is None else ps[:, 2 + rot % 2, :]
                if kind == "th":
                    i = op[1]
                    dve.wait_ge(done["th"], n)
                    j = 0 if i == 0 else (i - 1) % 2
                    if i in (1, 2):
                        dve.wait_ge(done["qs"], 2)
                    elif i > 2:
                        dve.wait_ge(done["q"], KC // 2 * ((i - 1) // 2))
                    dve.tensor_tensor(hT[:, :, j * P:(j + 1) * P], ps[:, 0:2, :].rearrange("p b (c t) -> p (b c) t", t=P),
                                      bcast(gx, P), ALU.mult).then_inc(t_ok, 1)
                    if i + 1 < NT:
                        scale(i + 1)
                elif kind == "tp":
                    dve.wait_ge(done["tp"], n)
                    s, j = op[1], op[2]
                    if s:
                        dve.wait_ge(done["oT"], KC // 2 * s)
                    dve.tensor_copy(pT[:, :, j * P:(j + 1) * P],
                                    ps[:, 0:2, :].rearrange("p b (c t) -> p (b c) t", t=P)).then_inc(t_ok, 1)
                elif kind == "oT":
                    s, c = op[1], op[2]
                    dve.wait_ge(done["oT"], n)
                    if s:
                        dve.wait_ge(done["out"], 4 * s)
                    dve.tensor_copy(oT[:, 2 * c:2 * c + 2, :], bank.rearrange("p (c t) -> p c t", t=PAIR)).then_inc(
                        rot_ok[rot % 2], 1)
                elif kind == "out":
                    s, j, h = op[1:]
                    dve.wait_ge(done["out"], n)
                    x = X[:, 2 * s + j, h * 512:(h + 1) * 512]
                    dve.tensor_tensor(x, x, bank, ALU.add).then_inc(rot_ok[rot % 2], 1)
                elif kind == "outs":
                    dve.wait_ge(done["outs"], n)
                    x = X[0:ROWS_S, TS, op[1] * 512:(op[1] + 1) * 512]
                    dve.tensor_tensor(x, x, bank[0:ROWS_S, :], ALU.add).then_inc(rot_ok[rot % 2], 1)
                elif kind == "sc":
                    j = op[2]
                    softmax(SOFT[op], ps[:, 4 + 2 * j:6 + 2 * j, :].rearrange("p b (h m) -> p (b h) m", m=NM),
                            E[:, j, :].rearrange("p (h m) -> p h m", m=NM), XH, (done["sc"], n), p_ok)
                elif kind == "ts":
                    softmax(SOFT[op], ps[0:ROWS_S, 6:8, :].rearrange("p b (h m) -> p (b h) m", m=NM),
                            ES[:, :].rearrange("p (h m) -> p h m", m=NM), XH, (done["kv"], NB), ES_ok)

        @block.tensor
        def _(pe):
            for op, n, rot in plan:
                kind = op[0]
                if kind == "ts":
                    continue
                if rot is not None:
                    bank = ps[:, 2 + rot % 2, :]
                    if rot >= 2:
                        pe.wait_ge(rot_ok[rot % 2], rot // 2)
                if kind in ("th", "tp") and TPOS[op]:
                    pe.wait_ge(t_ok, TPOS[op])
                if kind == "th":
                    pe.wait_ge(xs_ok, op[1] + 1)
                    for c in range(KC):
                        last = pe.transpose(ps[:, c // 4, c % 4 * P:(c % 4 + 1) * P], xs[:, c * P:(c + 1) * P], ident[:, :])
                elif kind == "tp":
                    pe.wait_ge(p_ok, 2 * op[1] + op[2] + 1)
                    for c in range(KC):
                        last = pe.transpose(ps[:, c // 4, c % 4 * P:(c % 4 + 1) * P], E[:, op[2], c * P:(c + 1) * P],
                                            ident[:, :])
                elif kind == "qs":
                    pe.wait_ge(keep["wkq_ld"], 16)
                    pe.wait_ge(t_ok, TPOS[("th", 0)] + 1)
                    for k in range(KC):
                        last = pe.matmul(bank[0:ROWS_S, :], hT[:, k, 0:ROWS_S], w_q[:, k, op[1] * 512:(op[1] + 1) * 512],
                                         start=(k == 0), stop=(k == KC - 1))
                elif kind == "qst":
                    read_out(pe, lambda o: o[0] == "qs")
                    for c in range(KC):
                        last = pe.transpose(bank[:, c * ROWS_S:(c + 1) * ROWS_S], E[0:ROWS_S, 0, c * P:(c + 1) * P],
                                            ident[0:ROWS_S, 0:ROWS_S])
                elif kind == "q":
                    pe.wait_ge(t_ok, TPOS[("th", 2 * op[1] + 2)] + 1)
                    for i in range(2):
                        c = 2 * op[2] + i
                        for k in range(KC):
                            last = pe.matmul(bank[:, i * PAIR:(i + 1) * PAIR], w_q[:, k, c * P:(c + 1) * P], hT[:, k, :],
                                             start=(k == 0), stop=(k == KC - 1))
                elif kind == "sc":
                    s, j = op[1], op[2]
                    read_out(pe, lambda o: o[0] == "q" and o[1] == s)
                    if s:
                        pe.wait_ge(exp_ok, SOFT[("sc", s - 1, j)] + 1)
                    elif j:
                        pe.wait_ge(exp_ok, SOFT[("ts",)] + 1)
                    for h in range(XH):
                        for dc in range(DC):
                            last = pe.matmul(ps[:, 4 + 2 * j + h // 2, h % 2 * NM:(h % 2 + 1) * NM],
                                             qT[:, 2 * h + dc, j * P:(j + 1) * P], KT[:, 2 * h + dc, :],
                                             start=(dc == 0), stop=(dc == DC - 1))
                elif kind == "oT":
                    pe.wait_ge(t_ok, TPOS[("tp", op[1], 1)] + 1)
                    for i in range(2):
                        c = 2 * op[2] + i
                        for mc in range(MC):
                            last = pe.matmul(bank[:, i * PAIR:(i + 1) * PAIR], V[:, mc, c * P:(c + 1) * P],
                                             pT[:, c // DC * MC + mc, :], start=(mc == 0), stop=(mc == MC - 1))
                elif kind == "out":
                    s, j, h = op[1:]
                    if (s, j, h) == (0, 0, 0):
                        pe.wait_ge(wo_ld, 16)
                    read_out(pe, lambda o: o[0] == "oT" and o[1] == s)
                    for c in range(KC):
                        last = pe.matmul(bank, oT[:, c, j * P:(j + 1) * P], w_o[:, c, h * 512:(h + 1) * 512],
                                         start=(c == 0), stop=(c == KC - 1))
                elif kind == "kv":
                    i = op[1]
                    pe.wait_ge(kv_ld[i % NRING], 16 * (i // NRING + 1))
                    if i == 0:
                        read_out(pe, lambda o: o[0] == "qst")
                    if i < NB:
                        kc = ring[:, i % NRING, :].rearrange("p (c m) -> p c m", c=KC)
                        for h in range(XH):
                            for dc in range(DC):
                                last = pe.matmul(ps[0:ROWS_S, 6 + h // 2, h % 2 * NM:(h % 2 + 1) * NM],
                                                 qSm[:, 2 * h + dc, i, :], kc[:, 2 * h + dc, :],
                                                 start=(i == 0 and h % 2 + dc == 0),
                                                 stop=(i == NB - 1 and h % 2 + dc == DC))
                    else:
                        b = i - NB
                        if b == 0:
                            read_out(pe, lambda o: o[0] == "tps")
                        vc = ring[:, i % NRING, :].rearrange("p (m n) -> p m n", m=MC)
                        for c in range(KC):
                            for mc in range(MC):
                                last = pe.matmul(bank[:, c * NL:(c + 1) * NL], vc[:, mc, c * P:(c + 1) * P],
                                                 pS[:, c // DC * MC + mc, b * NL:(b + 1) * NL], start=(mc == 0), stop=(mc == MC - 1))
                elif kind == "tps":
                    pe.wait_ge(ES_ok, 1)
                    for c in range(KC):
                        last = pe.transpose(bank[:, c * ROWS_S:(c + 1) * ROWS_S], ES[:, c * P:(c + 1) * P],
                                            ident[0:ROWS_S, 0:ROWS_S])
                elif kind == "outs":
                    if op[1] == 0:
                        read_out(pe, lambda o: o[0] == "kv" and o[1] >= NB)
                    for c in range(KC):
                        last = pe.matmul(bank[0:ROWS_S, :], oS[:, c, :], w_o[:, c, op[1] * 512:(op[1] + 1) * 512],
                                         start=(c == 0), stop=(c == KC - 1))
                last.then_inc(done[kind], 1)


def routing_buffers(nc, top, keep):
    def sb(name, shape):
        nonlocal top
        top -= -(-int(np.prod(shape[1:])) * 4 // 64) * 64
        keep[name] = nc.alloc_sbuf_tensor_at("r_" + name, shape, F32, offset=top)
    sb("gffn", [P, D])
    sb("wr", [P, KC, NL2])
    sb("brow", [1, NL2])
    sb("before", [P, P])
    sb("cst", [P, 4 + NT + NTILE + P])
    sb("tok", [P, 2, NT])
    keep["rc_ld"] = Sems(nc, keep["all"], "r")("c_ld")


def load_routing_buffers(sp, io, keep):
    consts = [(keep["gffn"][:, :], io["g_ffn"].to_broadcast([P, D])), (keep["wr"][:, :, :], io["w_r"]),
              (keep["brow"][:, :], io["b_r"]), (keep["before"][:, :], io["before"]),
              (keep["cst"][:, :], io["cst"].to_broadcast([P, 4 + NT + NTILE + P])), (keep["tok"][:, :, :], io["tok"])]
    for dst, src in consts:
        sp.dma_start(dst, src).then_inc(keep["rc_ld"], 16)
    keep["routing_loads"] = len(consts)


def routing_block(nc, io, keep, h_dram):
    with ExitStack() as ctx:
        sem = Sems(nc, keep["all"], "r")
        sb = lambda n, s, d=F32: ctx.enter_context(nc.sbuf_tensor("r_" + n, s, d))
        X, ps, ident, nhalf = keep["x"], keep["ps"], keep["ident"], keep["nhalf"]
        POS, WT, IDX, TAB = (keep[n] for n in ("pos", "wt", "idx", "tab"))
        K2 = 2 * NT
        NTHR = NT
        AHEAD, XB = 3, 3
        BT = lambda n: slice(6, 8) if n % 2 else slice(0, 2)
        gffn, wr, brow, before, cst, tok, c_ld = (keep[n] for n in ("gffn", "wr", "brow", "before", "cst", "tok", "rc_ld"))
        ones = sb("ones", [P, P])
        xs = sb("xs", [P, XB, D])
        hT = [sb(f"hT{i}", [P, KC, P]) for i in range(2)]
        junk = sb("junk", [P, D], BF16)
        st = sb("st", [P, 4 * NT])
        GL, EL = sb("GL", [P, NT, EG]), sb("EL", [P, NT, EG, EE])
        t4a, t4b, G1, d4, sel, sel2 = (sb(n, [P, NT, 4]) for n in ("t4a", "t4b", "G1", "d4", "sel", "sel2"))
        H = sb("H", [P, 2, NT, EE])
        m = {n: sb(n, [P, NT]) for n in ("gmax", "gsum", "gp", "km", "m1", "m2", "dm", "ex", "den", "rden")}
        prod = sb("prod", [P, NT, EG, EE])
        M = sb("M", [P, 2, NT, NE])
        Ms = sb("Ms", [P, NT, NE])
        tot = sb("tot", [P, NT, NE])
        run = sb("run", [P, NT + 1, NE])
        rank = sb("rank", [P, NT, NE])
        big = sb("big", [P, K2, P])
        cmp9 = sb("cmp9", [P, NE, NTHR])
        tl, ea, eb, base = (sb(n, [P, NE]) for n in ("tl", "ea", "eb", "base"))
        rk, bk, fl, rr, tt, pf = (sb(n, [P, K2]) for n in ("rk", "bk", "fl", "rr", "tt", "pf"))
        cmp8 = sb("cmp8", [P, K2, NTHR - 1])
        A = sb("A", [P, K2, NTILE])
        te, te2, base2 = sb("te", [P, NTILE, NE]), sb("te2", [P, NTILE, NE]), sb("base2", [P, NE])
        tef = sb("tef", [P, NTILE])
        first, started, used = sb("first", [P, NTILE]), sb("started", [P, NTILE]), sb("used", [P, NE])
        tt32 = sb("tt32", [P, NTILE, NTILE])
        ones_ok, h_st = sem("ones_ok"), sem("h_st", XB)
        sq_ok, r_ok, xs_ok, tr_ps, hT_ok, lg_ps, lg_ok = (
            sem(n) for n in ("sq_ok", "r_ok", "xs_ok", "tr_ps", "hT_ok", "lg_ps", "lg_ok"))
        step_ok, gd_ok, ge_ok, dm_ok, ex_ok, M_ok, cnt_ps, AB_ok, idx_ps = (
            sem(n) for n in ("step_ok", "gd_ok", "ge_ok", "dm_ok", "ex_ok", "M_ok", "cnt_ps", "AB_ok", "idx_ps"))
        tab_ok, lgT_ok, lgt_ps = sem("tab_ok"), sem("lgT_ok"), sem("lgt_ps")
        lgT = sb("lgT", [NL2, NT, P])
        tl0, row0 = sb("tl0", [P, 1]), sb("row0", [P, 1], I32)
        fall4 = cst[:, 0:4]
        thr = cst[:, 4:4 + NTHR]
        itile = cst[:, 4 + NTHR:4 + NTHR + NTILE]
        irow = cst[:, 4 + NTHR + NTILE:]
        block = ctx.enter_context(nc.Block())

        @block.sync
        def _(sp):
            for n in range(NT):
                sp.wait_ge(xs_ok, n + 1)
                sp.dma_start(h_dram[n * P:(n + 1) * P, :], xs[:, n % XB, :]).then_inc(h_st[n % XB], 16)
            for b in range(XB):
                sp.wait_ge(h_st[b], 16 * len(range(b, NT, XB)))
            sp.wait_ge(tab_ok, 1)
            row = sp.value_load(row0[0:1, 0:1], min_val=0, max_val=(NE - 1) * P)
            for p in range(3):
                sp.dma_start(keep["raw"][:, p, :], io["w_e"][ds(row, P), p * FC * D:(p + 1) * FC * D]).then_inc(
                    keep["w_ld"][p], 16)

        @block.gpsimd
        def _(pool):
            pool.memset(ones[:, :], 1.0).then_inc(ones_ok, 1)
            for n in range(NT):
                pool.wait_ge(sq_ok, n + 1)
                pool.tensor_scalar(st[:, 4 * n + 1:4 * n + 2], st[:, 4 * n:4 * n + 1], 1.0 / D, EPS, ALU.mult,
                                   ALU.add).then_inc(r_ok, 1)
                pool.wait_ge(r_ok, 2 * n + 1)
                pool.tensor_tensor(st[:, 4 * n + 2:4 * n + 3], st[:, 4 * n + 1:4 * n + 2], nhalf[:, :],
                                   ALU.pow).then_inc(r_ok, 1)

        @block.scalar
        def _(act):
            def square(n):
                if n:
                    act.wait_ge(sq_ok, n)
                act.activation(junk[:, :], X[:, n, :], ACT.Square, accum_out=st[:, 4 * n:4 * n + 1]).then_inc(sq_ok, 1)

            def copy_logits(n):
                act.wait_ge(lg_ps, n + 1)
                act.copy(lgT[:, n, :], ps[0:NL2, 2 + n % 3, 0:P]).then_inc(lgT_ok, 1)

            for n in range(AHEAD):
                square(n)
            for n in range(NT):
                if n + AHEAD < NT:
                    square(n + AHEAD)
                act.wait_ge(tr_ps, n + 1)
                if n >= 2:
                    act.wait_ge(lg_ps, n - 1)
                act.copy(hT[n % 2][:, :, :], ps[:, BT(n), :].rearrange("p b (c t) -> p (b c) t", t=P)).then_inc(hT_ok, 1)
                if n >= 2:
                    copy_logits(n - 2)
            copy_logits(NT - 2)
            copy_logits(NT - 1)
            act.wait_ge(gd_ok, 1)
            act.activation(t4b[:, :, :], d4[:, :, :], ACT.Exp).then_inc(ge_ok, 1)
            act.wait_ge(dm_ok, 1)
            act.activation(m["ex"][:, :], m["dm"][:, :], ACT.Exp).then_inc(ex_ok, 1)

        @block.tensor
        def _(pe):
            def logits(n):
                pe.wait_ge(hT_ok, n + 1)
                if n >= 3:
                    pe.wait_ge(lgT_ok, n - 2)
                out = ps[0:NL2, 2 + n % 3, 0:P]
                for c in range(KC):
                    pe.matmul(out, wr[:, c, :], hT[n % 2][:, c, :], start=(c == 0), stop=False)
                pe.matmul(out, brow[:, :], ones[0:1, :], start=False, stop=True).then_inc(lg_ps, 1)

            def turn_logits(n):
                pe.wait_ge(lgT_ok, n + 1)
                pe.transpose(ps[:, 5, n * NL2:(n + 1) * NL2], lgT[:, n, :], ident[0:NL2, 0:NL2]).then_inc(lgt_ps, 1)

            pe.wait_ge(c_ld, 16 * keep["routing_loads"])
            pe.wait_ge(ones_ok, 1)
            for n in range(NT):
                pe.wait_ge(xs_ok, n + 1)
                if n >= 2:
                    pe.wait_ge(hT_ok, n - 1)
                for c in range(KC):
                    last = pe.transpose(ps[:, BT(n).start + c // 4, c % 4 * P:(c % 4 + 1) * P], xs[:, n % XB, c * P:(c + 1) * P],
                                        ident[:, :])
                last.then_inc(tr_ps, 1)
                if n:
                    logits(n - 1)
                if n >= 3:
                    turn_logits(n - 3)
            logits(NT - 1)
            for n in range(NT - 3, NT):
                turn_logits(n)
            pe.wait_ge(M_ok, 1)
            Mf = Ms[:, :, :].rearrange("p t e -> p (t e)")
            pe.matmul(ps[:, 3, 0:NT * NE], before[:, :], Mf, start=True, stop=True)
            pe.matmul(ps[:, 4, 0:NT * NE], ones[:, :], Mf, start=True, stop=True).then_inc(cnt_ps, 1)
            pe.wait_ge(AB_ok, 1)
            for i in range(K2):
                last = pe.matmul(ps[:, 5, 0:NTILE], big[:, i, :], A[:, i, :], start=(i == 0), stop=(i == K2 - 1))
            last.then_inc(idx_ps, 1)

        @block.vector
        def _(dve):
            dve.wait_ge(c_ld, 16 * keep["routing_loads"])
            for n in range(NT):
                dve.wait_ge(r_ok, 2 * n + 2)
                if n >= XB:
                    dve.wait_ge(tr_ps, n - XB + 1)
                    dve.wait_ge(h_st[n % XB], 16 * (n // XB))
                dve.scalar_tensor_tensor(out=xs[:, n % XB, :], in0=X[:, n, :], scalar=st[:, 4 * n + 2:4 * n + 3],
                                         in1=gffn[:, :], op0=ALU.mult, op1=ALU.mult).then_inc(xs_ok, 1)
            count = [0]

            def then(ins):
                count[0] += 1
                ins.then_inc(step_ok, 1)
                dve.wait_ge(step_ok, count[0])

            v, r = dve.tensor_tensor, dve.tensor_reduce
            dve.wait_ge(lgt_ps, NT)
            lg = ps[:, 5, 0:NT * NL2].rearrange("p (t n) -> p t n", n=NL2)
            dve.tensor_copy(EL[:, :, :, :].rearrange("p t g e -> p t (g e)"), lg[:, :, EG:NL2])
            then(dve.tensor_copy(GL[:, :, :], lg[:, :, 0:EG]))
            then(r(m["gmax"][:, :], GL[:, :, :], AX_X, ALU.max))
            v(d4[:, :, :], GL[:, :, :], bcast(m["gmax"][:, :], 4), ALU.subtract).then_inc(gd_ok, 1)
            f4 = fall4.rearrange("p (o n) -> p o n", o=1).to_broadcast([P, NT, 4])

            def first_of(out, x, top):
                then(v(t4a[:, :, :], x, bcast(top, 4), ALU.is_equal))
                then(v(t4a[:, :, :], t4a[:, :, :], f4, ALU.mult))
                then(r(m["km"][:, :], t4a[:, :, :], AX_X, ALU.max))
                then(v(out, t4a[:, :, :], bcast(m["km"][:, :], 4), ALU.is_equal))

            first_of(G1[:, :, :], GL[:, :, :], m["gmax"][:, :])
            dve.wait_ge(ge_ok, 1)
            then(r(m["gsum"][:, :], t4b[:, :, :], AX_X, ALU.add))
            then(dve.reciprocal(m["gp"][:, :], m["gsum"][:, :]))
            g1e = G1[:, :, :].rearrange("p t (g o) -> p t g o", o=1).to_broadcast([P, NT, EG, EE])
            then(v(prod[:, :, :, :], EL[:, :, :, :], g1e, ALU.mult))
            then(r(sel[:, :, :], prod[:, :, :, :].rearrange("p t g e -> p t e g"), AX_X, ALU.add))
            then(r(m["m1"][:, :], sel[:, :, :], AX_X, ALU.max))
            first_of(H[:, 0, :, :], sel[:, :, :], m["m1"][:, :])
            then(dve.scalar_tensor_tensor(out=sel2[:, :, :], in0=H[:, 0, :, :], scalar=-3.0e38, in1=sel[:, :, :],
                                          op0=ALU.mult, op1=ALU.add))
            then(r(m["m2"][:, :], sel2[:, :, :], AX_X, ALU.max))
            first_of(H[:, 1, :, :], sel2[:, :, :], m["m2"][:, :])
            v(m["dm"][:, :], m["m2"][:, :], m["m1"][:, :], ALU.subtract).then_inc(dm_ok, 1)
            dve.wait_ge(ex_ok, 1)
            then(dve.tensor_scalar(m["den"][:, :], m["ex"][:, :], 1.0, None, ALU.add))
            then(dve.reciprocal(m["rden"][:, :], m["den"][:, :]))
            then(v(WT[:, 0, :], m["gp"][:, :], m["rden"][:, :], ALU.mult))
            then(v(WT[:, 1, :], WT[:, 0, :], m["ex"][:, :], ALU.mult))
            then(v(G1[:, :, :], G1[:, :, :], bcast(tok[:, 1, :], 4), ALU.mult))
            for k in range(2):
                for g in range(EG):
                    last = v(M[:, k, :, g * EE:(g + 1) * EE], H[:, k, :, :],
                             G1[:, :, g:g + 1].to_broadcast([P, NT, EE]), ALU.mult)
            then(last)
            v(Ms[:, :, :], M[:, 0, :, :], M[:, 1, :, :], ALU.add).then_inc(M_ok, 1)
            dve.wait_ge(cnt_ps, 1)
            dve.memset(run[:, 0, :], 0.0)
            then(dve.tensor_copy(tot[:, :, :], ps[:, 4, 0:NT * NE].rearrange("p (t e) -> p t e", e=NE)))
            for t in range(NT):
                then(v(run[:, t + 1, :], run[:, t, :], tot[:, t, :], ALU.add))
            then(v(rank[:, :, :], run[:, 0:NT, :], ps[:, 3, 0:NT * NE].rearrange("p (t e) -> p t e", e=NE), ALU.add))
            then(v(cmp9[:, :, :], bcast(run[:, NT, :], NTHR), thr.rearrange("p (o n) -> p o n", o=1).to_broadcast(
                [P, NE, NTHR]), ALU.is_gt))
            then(r(tl[:, :], cmp9[:, :, :], AX_X, ALU.add))
            then(dve.tensor_copy(ea[:, :], tl[:, :]))
            src, dst = ea, eb
            for k in (1, 2, 4, 8):
                dve.tensor_copy(dst[:, 0:k], src[:, 0:k])
                then(v(dst[:, k:NE], src[:, k:NE], src[:, 0:NE - k], ALU.add))
                src, dst = dst, src
            end = src
            then(v(base[:, :], end[:, :], tl[:, :], ALU.subtract))
            then(dve.tensor_scalar(used[:, :], end[:, :], 0.0, None, ALU.is_equal))
            then(r(tl0[:, :], used[:, :], AX_X, ALU.add))
            then(dve.tensor_scalar(row0[:, :], tl0[:, :], float(P), None, ALU.mult))
            dve.sem_inc(tab_ok, 1)
            for k in range(2):
                then(v(prod[:, :, :, :].rearrange("p t g e -> p t (g e)"), M[:, k, :, :], rank[:, :, :], ALU.mult))
                then(r(rk[:, k * NT:(k + 1) * NT], prod[:, :, :, :].rearrange("p t g e -> p t (g e)"), AX_X, ALU.add))
                then(v(prod[:, :, :, :].rearrange("p t g e -> p t (g e)"), M[:, k, :, :],
                       base[:, :].rearrange("p (o e) -> p o e", o=1).to_broadcast([P, NT, NE]), ALU.mult))
                then(r(bk[:, k * NT:(k + 1) * NT], prod[:, :, :, :].rearrange("p t g e -> p t (g e)"), AX_X, ALU.add))
            then(v(cmp8[:, :, :], bcast(rk[:, :], NTHR - 1), thr[:, 1:NTHR].rearrange("p (o n) -> p o n", o=1).to_broadcast(
                [P, K2, NTHR - 1]), ALU.is_ge))
            then(r(fl[:, :], cmp8[:, :, :], AX_X, ALU.add))
            dve.scalar_tensor_tensor(out=rr[:, :], in0=fl[:, :], scalar=-float(P), in1=rk[:, :], op0=ALU.mult, op1=ALU.add)
            then(v(tt[:, :], bk[:, :], fl[:, :], ALU.add))
            then(dve.scalar_tensor_tensor(out=pf[:, :], in0=tt[:, :], scalar=float(P), in1=rr[:, :], op0=ALU.mult,
                                          op1=ALU.add))
            then(dve.tensor_copy(POS[:, :], pf[:, :]))
            v(big[:, :, :], bcast(rr[:, :], P), irow.rearrange("p (o n) -> p o n", o=1).to_broadcast([P, K2, P]),
              ALU.is_equal)
            then(v(A[:, :, :], bcast(tt[:, :], NTILE), itile.rearrange("p (o n) -> p o n", o=1).to_broadcast(
                [P, K2, NTILE]), ALU.is_equal))
            for k in range(2):
                last = v(A[:, k * NT:(k + 1) * NT, :], A[:, k * NT:(k + 1) * NT, :], bcast(tok[:, 0, :], NTILE), ALU.mult)
            last.then_inc(AB_ok, 1)
            then(dve.tensor_scalar(used[:, :], tl[:, :], 0.0, float(2 * NTILE), ALU.is_equal, ALU.mult))
            then(v(base2[:, :], base[:, :], used[:, :], ALU.add))
            over = lambda x: x.rearrange("p (o e) -> p o e", o=1).to_broadcast([P, NTILE, NE])
            then(v(te[:, :, :], over(base2[:, :]), bcast(itile, NE), ALU.is_le))
            r(started[:, :], te[:, :, :], AX_X, ALU.add)
            then(v(te2[:, :, :], te[:, :, :], over(itile[:, 0:NE]), ALU.mult))
            r(tef[:, :], te2[:, :, :], AX_X, ALU.max)
            dve.tensor_copy(first[:, 0:1], started[:, 0:1])
            then(v(first[:, 1:NTILE], started[:, 1:NTILE], started[:, 0:NTILE - 1], ALU.subtract))
            dve.tensor_scalar(TAB[:, 1, :], tef[:, :], float(P), None, ALU.mult)
            then(v(TAB[:, 0, :], started[:, :], first[:, :], ALU.mult))
            then(dve.tensor_scalar(tef[:, :], started[:, :], -1.0, None, ALU.add))
            then(v(tt32[:, :, :], bcast(tef[:, :], NTILE), started[:, :].rearrange("p (o n) -> p o n", o=1).to_broadcast(
                [P, NTILE, NTILE]), ALU.is_gt))
            then(r(tef[:, :], tt32[:, :, :], AX_X, ALU.add))
            then(dve.tensor_scalar(TAB[:, 3, :], tef[:, :], 1.0, None, ALU.add))
            then(v(tef[:, :], end[:, NE - 1:NE].to_broadcast([P, NTILE]), itile, ALU.is_gt))
            then(v(TAB[:, 2, :], started[:, :], tef[:, :], ALU.mult))
            then(r(used[:, 0:2], tef[:, :].rearrange("p (t o) -> p o t", o=2), AX_X, ALU.add))
            then(dve.tensor_scalar(TAB[:, 4, 0:2], used[:, 0:2], 16.0, None, ALU.mult))
            dve.wait_ge(idx_ps, 1)
            dve.tensor_copy(IDX[:, :], ps[:, 5, 0:NTILE])


def split_product(pe, out, pairs):
    for n, ((xh, xl), (wh, wl)) in enumerate(pairs):
        pe.matmul(out, xh, wh, start=(n == 0), stop=False)
        pe.matmul(out, xh, wl, start=False, stop=False)
        last = pe.matmul(out, xl, wh, start=False, stop=(n == len(pairs) - 1))
    return last


def experts_block(nc, io, keep, h_dram, y_dram):
    PIECE = FC * D
    assert 2 * PIECE == KC * 2 * FE
    with ExitStack() as ctx:
        sem = Sems(nc, keep["all"], "e")
        sb = lambda n, s, d=F32: ctx.enter_context(nc.sbuf_tensor("e_" + n, s, d))
        ps, ident, IDX, TAB = (keep[n] for n in ("ps", "ident", "idx", "tab"))
        Wh, Wl = sb("Wh", [P, 2 * ESZ], F32R), sb("Wl", [P, 2 * ESZ], F32R)
        raw, w_ld = keep["raw"], keep["w_ld"]
        xg = sb("xg", [P, 2, D])
        xTh, xTl = ([sb(f"xT{n}{i}", [P, KC, P], F32R) for i in range(2)] for n in "hl")
        aTh, aTl = ([sb(f"aT{n}{i}", [P, FC, P], F32R) for i in range(2)] for n in "hl")
        sg, a = sb("sg", [P, FE]), sb("a", [P, FE])
        y = sb("y", [P, 2, D])
        x_ld, y_st = sem("x_ld", 2), sem("y_st", 2)
        hi_ok, lo_ok = sem("hi_ok", 3), sem("lo_ok", 3)
        tr_ps, xTh_ok, xT_ok, gu_ps, sg_ok, a_ok, aT_ps, aTh_ok, aT_ok, dn_ps, y_ok = (
            sem(n) for n in ("tr_ps", "xTh_ok", "xT_ok", "gu_ps", "sg_ok", "a_ok", "aT_ps", "aTh_ok", "aT_ok", "dn_ps",
                             "y_ok"))
        block = ctx.enter_context(nc.Block())

        def starts(eng, j):
            return eng.value_load(TAB[0:1, 0, ds(j, 1)], min_val=0, max_val=NE)

        def started(eng, j):
            return eng.value_load(TAB[0:1, 2, ds(j, 1)], min_val=0, max_val=NE)

        def buffer(n):
            return (n + 1) % 2 * ESZ

        def tile_steps(eng, emit):
            def unless_empty(s, like):
                with eng.If(started(eng, s - 1) >= 1):
                    emit(s, like)
            for s in range(4):
                emit(s, s)
            for lo, hi, each in ((4, MIN_TILES - 1, emit), (MIN_TILES - 1, NTILE - 2, unless_empty)):
                with eng.Fori(0, (hi - lo) // 2) as i:
                    for u in range(2):
                        each(2 * i + (lo + u), 4 + u)
            for s in range(NTILE - 2, NTILE + 1):
                unless_empty(s, s)

        @block.sync
        def _(sp):
            with sp.Fori(1, NTILE) as j:
                n = starts(sp, j)
                with sp.If(n >= 1):
                    row = sp.value_load(TAB[0:1, 1, ds(j, 1)], min_val=0, max_val=(NE - 1) * P)
                    for p, at in ((0, 0), (1, PIECE), (2, 2 * PIECE)):
                        sp.wait_ge(lo_ok[p], n)
                        sp.dma_start(raw[:, p, :], io["w_e"][ds(row, P), at:at + PIECE]).then_inc(w_ld[p], 16)

        @block.gpsimd
        def _(pool):
            def fetch(j):
                if j >= 2:
                    pool.wait_ge(tr_ps, j - 1)
                pool.indirect_dma_start(xg[:, j % 2, :], None, h_dram[:, :],
                                        bass.IndirectOffsetOnAxis(ap=IDX[:, j:j + 1], axis=0)).then_inc(x_ld[j % 2], 16)
            for j in range(NTILE):
                if j < MIN_TILES + 2:
                    fetch(j)
                else:
                    with pool.If(started(pool, j - 2) >= 1):
                        fetch(j)

        @block.scalar
        def _(act):
            def round_piece(j, p):
                n = starts(act, j)
                with act.If(n >= 1):
                    free = act.value_load(TAB[0:1, 3, ds(j, 1)], min_val=1, max_val=NTILE + 1)
                    off = buffer(n)
                    for q in p:
                        act.wait_ge(w_ld[q], 16 * n)
                        if q == 2:
                            act.wait_ge(dn_ps, 2 * free)
                        else:
                            act.wait_ge(gu_ps, free)
                        act.copy(Wh[:, ds(off + q * PIECE, PIECE)], raw[:, q, :]).then_inc(hi_ok[q], 1)

            def round_xT(j, like):
                act.wait_ge(tr_ps, j + 1)
                if like >= 2:
                    act.wait_ge(gu_ps, j)
                act.copy(xTh[like % 2][:, :, :], ps[:, 0:2, :].rearrange("p b (c t) -> p (b c) t", t=P)).then_inc(
                    xTh_ok, 1)

            round_piece(0, (0, 1))
            round_xT(0, 0)
            round_piece(0, (2,))
            round_piece(1, (0, 1))

            def step(s, like):
                if like + 1 < NTILE:
                    round_xT(s + 1, like + 1)
                if like < NTILE:
                    act.wait_ge(gu_ps, s + 2)
                    if like >= 1:
                        act.wait_ge(a_ok, s)
                    act.activation(sg[:, :], ps[:, 2 + like % 2, 0:FE], ACT.Silu).then_inc(sg_ok, 1)
                if like + 2 < NTILE:
                    round_piece(s + 2, (0,))
                if like < NTILE:
                    act.wait_ge(aT_ps, s + 1)
                    if like >= 2:
                        act.wait_ge(dn_ps, 2 * (s - 1) + 2)
                    act.copy(aTh[like % 2][:, :, :], ps[:, 6, 0:FC * P].rearrange("p (c t) -> p c t", t=P)).then_inc(
                        aTh_ok, 1)
                if like + 2 < NTILE:
                    round_piece(s + 2, (1,))
                if like >= 1:
                    par = (like - 1) % 2
                    act.wait_ge(dn_ps, 2 * (s - 1) + 3)
                    if like >= 3:
                        act.wait_ge(y_st[par], 8 * (s - 1 - par))
                    act.copy(y[:, par, 0:512], ps[:, 4, :]).then_inc(y_ok, 1)
                    act.wait_ge(dn_ps, 2 * (s - 1) + 4)
                    act.copy(y[:, par, 512:D], ps[:, 5, :]).then_inc(y_ok, 1)
                if like + 1 < NTILE:
                    round_piece(s + 1, (2,))
                if like >= 1:
                    act.wait_ge(y_ok, 2 * (s - 1) + 2)
                    act.dma_start(y_dram[ds((s - 1) * P, P), :], y[:, par, :]).then_inc(y_st[par], 16)
            tile_steps(act, step)
            stores = [act.value_load(TAB[0:1, 4, par:par + 1], min_val=16, max_val=8 * NTILE) for par in range(2)]
            for par in range(2):
                act.wait_ge(y_st[par], stores[par])
            act.copy(sg[0:1, 0:1], ident[0:1, 0:1])

        @block.vector
        def _(dve):
            def rest_of_piece(j, p):
                n = starts(dve, j)
                with dve.If(n >= 1):
                    off = buffer(n)
                    for q in p:
                        dve.wait_ge(hi_ok[q], n)
                        at = ds(off + q * PIECE, PIECE)
                        dve.tensor_tensor(Wl[:, at], raw[:, q, :], Wh[:, at].bitcast(F32), ALU.subtract).then_inc(
                            lo_ok[q], 1)

            def rest_of_xT(j, like):
                dve.wait_ge(xTh_ok, j + 1)
                dve.tensor_tensor(xTl[like % 2][:, :, :], ps[:, 0:2, :].rearrange("p b (c t) -> p (b c) t", t=P),
                                  xTh[like % 2][:, :, :].bitcast(F32), ALU.subtract).then_inc(xT_ok, 1)

            for q in range(3):
                dve.sem_inc(lo_ok[q], 1)
            rest_of_piece(0, (0, 1))
            rest_of_xT(0, 0)
            rest_of_piece(0, (2,))
            rest_of_piece(1, (0, 1))

            def step(s, like):
                if like + 1 < NTILE:
                    rest_of_xT(s + 1, like + 1)
                if like < NTILE:
                    dve.wait_ge(sg_ok, s + 1)
                    if like >= 1:
                        dve.wait_ge(aT_ps, s)
                    dve.tensor_tensor(a[:, :], sg[:, :], ps[:, 2 + like % 2, FE:2 * FE], ALU.mult).then_inc(a_ok, 1)
                if like + 2 < NTILE:
                    rest_of_piece(s + 2, (0,))
                if like < NTILE:
                    dve.wait_ge(aTh_ok, s + 1)
                    dve.tensor_tensor(aTl[like % 2][:, :, :], ps[:, 6, 0:FC * P].rearrange("p (c t) -> p c t", t=P),
                                      aTh[like % 2][:, :, :].bitcast(F32), ALU.subtract).then_inc(aT_ok, 1)
                if like + 2 < NTILE:
                    rest_of_piece(s + 2, (1,))
                if like + 1 < NTILE:
                    rest_of_piece(s + 1, (2,))
            tile_steps(dve, step)

        @block.tensor
        def _(pe):
            def turn(j, like):
                pe.wait_ge(x_ld[like % 2], 8 * (j - like % 2) + 16)
                if like >= 1:
                    pe.wait_ge(xT_ok, j)
                for c in range(KC):
                    last = pe.transpose(ps[:, c // 4, c % 4 * P:(c % 4 + 1) * P], xg[:, like % 2, c * P:(c + 1) * P],
                                        ident[:, :])
                last.then_inc(tr_ps, 1)

            def weights(off, at):
                return Wh[:, ds(off + at, 512)], Wl[:, ds(off + at, 512)]

            def gate_up(j, like, n):
                pe.wait_ge(xT_ok, j + 1)
                if like >= 2:
                    pe.wait_ge(a_ok, j - 1)
                pe.wait_ge(lo_ok[0], n + 1)
                pe.wait_ge(lo_ok[1], n + 1)
                off = buffer(n)
                split_product(pe, ps[:, 2 + like % 2, :],
                              [((xTh[like % 2][:, c, :], xTl[like % 2][:, c, :]), weights(off, c * 2 * FE))
                               for c in range(KC)]).then_inc(gu_ps, 1)

            def turn_a(j, like):
                pe.wait_ge(a_ok, j + 1)
                if like >= 1:
                    pe.wait_ge(aT_ok, j)
                for c in range(FC):
                    last = pe.transpose(ps[:, 6, c * P:(c + 1) * P], a[:, c * P:(c + 1) * P], ident[:, :])
                last.then_inc(aT_ps, 1)

            def down(j, like, n):
                pe.wait_ge(aT_ok, j + 1)
                pe.wait_ge(lo_ok[2], n + 1)
                off = buffer(n)
                for h in range(2):
                    if like >= 1:
                        pe.wait_ge(y_ok, 2 * j - 1 + h)
                    split_product(pe, ps[:, 4 + h, :],
                                  [((aTh[like % 2][:, c, :], aTl[like % 2][:, c, :]),
                                    weights(off, KC * 2 * FE + c * D + h * 512)) for c in range(FC)]).then_inc(dn_ps, 1)

            pe.sem_inc(gu_ps, 1)
            pe.sem_inc(dn_ps, 2)
            turn(0, 0)

            def step(s, like, last, this):
                if like + 1 < NTILE:
                    turn(s + 1, like + 1)
                if like < NTILE:
                    gate_up(s, like, this)
                if like >= 1:
                    down(s - 1, like - 1, last)
                if like < NTILE:
                    turn_a(s, like)

            this = None
            for s in range(4):
                last, this = this, started(pe, s)
                step(s, s, last, this)
            for lo, hi in ((4, MIN_TILES - 1), (MIN_TILES - 1, NTILE - 2)):
                with pe.Fori(0, (hi - lo) // 2) as i:
                    s = 2 * i + lo
                    n = [started(pe, s - 1), started(pe, s)]
                    with ExitStack() as maybe:
                        if lo > 4:
                            maybe.enter_context(pe.If(n[0] >= 1))
                        step(s, 4, n[0], n[1])
                        if lo > 4:
                            maybe.enter_context(pe.If(n[1] >= 1))
                        step(s + 1, 5, n[1], started(pe, s + 1))
            for s in range(NTILE - 2, NTILE + 1):
                last = started(pe, s - 1)
                with pe.If(last >= 1):
                    step(s, s, last, started(pe, s) if s < NTILE else None)


def combine_block(nc, io, keep, y_dram):
    with ExitStack() as ctx:
        sem = Sems(nc, keep["all"], "c")
        sb = lambda n, s, d=F32: ctx.enter_context(nc.sbuf_tensor("c_" + n, s, d))
        X, POS, WT, nhalf = (keep[n] for n in ("x", "pos", "wt", "nhalf"))
        NBF = 3
        gf = sb("gf", [P, D])
        o = sb("o", [P, NBF, D])
        yg = sb("yg", [P, NBF, 2, D])
        junk = sb("junk", [P, D], BF16)
        st = sb("st", [P, 4 * NT])
        g_ld, y_ld, o_st = sem("g_ld"), sem("y_ld", NBF), sem("o_st", NBF)
        x0_ok, x_ok, sq_ok, r_ok, o_ok = (sem(n) for n in ("x0_ok", "x_ok", "sq_ok", "r_ok", "o_ok"))
        block = ctx.enter_context(nc.Block())

        @block.sync
        def _(sp):
            sp.dma_start(gf[:, :], io["g_final"].to_broadcast([P, D])).then_inc(g_ld, 16)
            for t in range(NT):
                sp.wait_ge(o_ok, t + 1)
                if t < TS:
                    sp.dma_start(io["y_p"][t * P:(t + 1) * P, :], o[:, t % NBF, :]).then_inc(o_st[t % NBF], 16)
                else:
                    sp.dma_start(io["y_s"], o[0:ROWS_S, t % NBF, :]).then_inc(o_st[t % NBF], 16)
            for b in range(NBF):
                sp.wait_ge(o_st[b], 16 * len(range(b, NT, NBF)))

        @block.gpsimd
        def _(pool):
            def fetch(t):
                if t >= NBF:
                    pool.wait_ge(x_ok, t - NBF + 1)
                for k in range(2):
                    pool.indirect_dma_start(yg[:, t % NBF, k, :], None, y_dram[:, :],
                                            bass.IndirectOffsetOnAxis(ap=POS[:, k * NT + t:k * NT + t + 1], axis=0)
                                            ).then_inc(y_ld[t % NBF], 16)
            fetch(0)
            fetch(1)
            for n in range(NT):
                if n + 2 < NT:
                    fetch(n + 2)
                pool.wait_ge(sq_ok, n + 1)
                pool.tensor_scalar(st[:, 4 * n + 1:4 * n + 2], st[:, 4 * n:4 * n + 1], 1.0 / D, EPS, ALU.mult,
                                   ALU.add).then_inc(r_ok, 1)
                pool.wait_ge(r_ok, 2 * n + 1)
                pool.tensor_tensor(st[:, 4 * n + 2:4 * n + 3], st[:, 4 * n + 1:4 * n + 2], nhalf[:, :],
                                   ALU.pow).then_inc(r_ok, 1)

        @block.scalar
        def _(act):
            for t in range(NT):
                act.wait_ge(x_ok, t + 1)
                if t:
                    act.wait_ge(sq_ok, t)
                act.activation(junk[:, :], X[:, t, :], ACT.Square, accum_out=st[:, 4 * t:4 * t + 1]).then_inc(sq_ok, 1)

        @block.vector
        def _(dve):
            def add(t):
                for k in range(2):
                    dve.wait_ge(y_ld[t % NBF], 32 * (t // NBF + 1))
                    if k:
                        dve.wait_ge(x0_ok, t + 1)
                    dve.scalar_tensor_tensor(out=X[:, t, :], in0=yg[:, t % NBF, k, :], scalar=WT[:, k, t:t + 1],
                                             in1=X[:, t, :], op0=ALU.mult, op1=ALU.add).then_inc(x_ok if k else x0_ok, 1)
            add(0)
            dve.wait_ge(g_ld, 16)
            for t in range(NT):
                if t + 1 < NT:
                    add(t + 1)
                dve.wait_ge(r_ok, 2 * t + 2)
                if t >= NBF:
                    dve.wait_ge(o_st[t % NBF], 16 * (t // NBF))
                dve.scalar_tensor_tensor(out=o[:, t % NBF, :], in0=X[:, t, :], scalar=st[:, 4 * t + 2:4 * t + 3],
                                         in1=gf[:, :], op0=ALU.mult, op1=ALU.mult).then_inc(o_ok, 1)


def build(nc, io):
    x1_dram = nc.dram_tensor("x1_rows", [NT * P, D], F32, kind="Internal").ap()
    h_dram = nc.dram_tensor("h_rows", [NT * P, D], F32, kind="Internal").ap()
    y_dram = nc.dram_tensor("y_rows", [NTILE * P, D], F32, kind="Internal").ap()
    with ExitStack() as ctx:
        sb = lambda c, n, s, d=F32: c.enter_context(nc.sbuf_tensor(n, s, d))
        keep = {"all": ctx}
        keep["ps"] = ctx.enter_context(nc.psum_tensor("ps", [P, 8, 512], F32))
        keep["ident"] = sb(ctx, "ident", [P, P])
        keep["nhalf"] = sb(ctx, "nhalf", [P, 1])
        keep["gcol"] = sb(ctx, "gcol", [P, 4 * KC + NG])
        keep["win_ld"] = ctx.enter_context(nc.semaphore("win_ld"))
        keep["wkq_ld"] = ctx.enter_context(nc.semaphore("wkq_ld"))
        keep["pos"] = sb(ctx, "pos", [P, 2 * NT], I32)
        keep["wt"] = sb(ctx, "wt", [P, 2, NT])
        keep["idx"] = sb(ctx, "idx", [P, NTILE], I32)
        keep["tab"] = sb(ctx, "tab", [P, 5, NTILE], I32)
        with ExitStack() as att:
            keep["V"] = sb(att, "V", [P, MC, D])
            keep["KT"] = sb(att, "KT", [P, KC, NM])
            keep["wkq"] = sb(att, "wkq", [P, KC, D])
            with ExitStack() as mix:
                keep["w_in"] = sb(mix, "w_in", [P, KC, 3 * WA])
                mixing_buffers(nc, mix, io, keep)
                memory_block(nc, io, keep)
                mixing_block(nc, io, keep, x1_dram)
            x_at = nc.sbuf_usable_end - NT * D * 4 - 64
            x_at -= x_at % 64
            keep["x"] = nc.alloc_sbuf_tensor_at("x", [P, NT, D], F32, offset=x_at)
            routing_buffers(nc, x_at, keep)
            attention_block(nc, io, keep, x1_dram, y_dram)
        keep["raw"] = sb(ctx, "raw", [P, 3, FC * D])
        keep["w_ld"] = [ctx.enter_context(nc.semaphore(f"w_ld{p}")) for p in range(3)]
        routing_block(nc, io, keep, h_dram)
        experts_block(nc, io, keep, h_dram, y_dram)
        combine_block(nc, io, keep, y_dram)


def kernel(**inputs):
    import concourse.bacc as bacc
    from concourse.bass_utils import run_bass_kernel_spmd

    np_in = {k: np.asarray(v) for k, v in inputs.items()}
    nc = bacc.Bacc("TRN2", target_bir_lowering=False, num_devices=1)
    arrays, io = {}, {}

    def give(name, a):
        a = np.ascontiguousarray(a)
        arrays["in_" + name] = a
        io[name] = nc.dram_tensor("in_" + name, a.shape, mybir.dt.from_np(a.dtype), kind="ExternalInput").ap()

    def chunks(w):
        return w.reshape(w.shape[0] // P, P, w.shape[1]).transpose(1, 0, 2)

    f = np.float32
    x = np.zeros((NT * P, D), f)
    x[0:SEQ] = np_in["x_prompt"][0]
    x[SEQ:SEQ + ROWS_S] = np_in["x_sample"].reshape(ROWS_S, D)
    give("x", x)
    give("mem", np_in["mem_prompt"][0])
    gcol = np.concatenate([np_in[n].reshape(KC, P).T for n in ("g_mem", "g_mix", "g_xattn", "g_ffn")]
                          + [np_in["s_pool"].reshape(NG, P).T], axis=1)
    give("gcol", gcol)
    for n in ("w_xk", "w_xv", "w_xq", "w_xo", "w_in", "w_out"):
        give(n, chunks(np_in[n][0]))
    w_s = np_in["w_s"][0]
    give("wsT", w_s.transpose(2, 0, 1))
    wsTs = np.zeros((ROWS_S, HA, ROWS_S), f)
    for b in range(NB):
        wsTs[b * NL:(b + 1) * NL, :, b * NL:(b + 1) * NL] = w_s[:, 0:NL, 0:NL].transpose(2, 0, 1)
    give("wsTs", wsTs)
    band, bandp = banded()
    give("band", band.transpose(1, 0, 2, 3))
    give("bandp", bandp.transpose(1, 0, 2, 3))
    give("w_pool", np_in["w_pool"][0].transpose(1, 0, 2))
    give("g_v", np_in["g_v"])
    b_s = np_in["b_s"][0]
    give("bias", np.concatenate([b_s] + [b_s[:, 0:NL]] * NB, axis=1))
    give("head_of", np.repeat(np.eye(HA, dtype=f), DHA, axis=1))
    hist = np.zeros((P, WA), f)
    hist[0:NB * HIST] = np_in["state_pool"][0].reshape(NB * HIST, WA)
    give("hist", hist)
    give("state", np_in["state_pool"][0])
    kc = np_in["cache_mem_k"][0].reshape(NB, NM, XH, DC, P).transpose(0, 4, 2, 3, 1)
    give("kc", kc.reshape(NB, P, 2 * D))
    vc = np_in["cache_mem_v"][0].reshape(NB, MC, P, D).transpose(0, 2, 1, 3)
    give("vc", vc.reshape(NB, P, 2 * D))
    give("g_ffn", np_in["g_ffn"])
    give("g_final", np_in["g_final"].reshape(1, D))
    give("w_r", chunks(np.concatenate([np_in["w_group"][0], np_in["w_router"][0]], axis=1)))
    give("b_r", np.concatenate([np_in["b_group"], np_in["b_router"]], axis=1))
    give("before", np.triu(np.ones((P, P), f), 1))
    give("cst", np.concatenate([np.arange(4, 0, -1), P * np.arange(NT), np.arange(NTILE), np.arange(P)]).astype(f)[None])
    real = (np.arange(NT * P) < SEQ + ROWS_S).astype(f)
    give("tok", np.stack([(np.arange(NT * P) * real).reshape(NT, P).T, real.reshape(NT, P).T], axis=1).astype(f))
    gu = np.concatenate([np_in["w_gate"][0], np_in["w_up"][0]], axis=2).reshape(NE, KC, P, 2 * FE).transpose(0, 2, 1, 3)
    dn = np_in["w_down"][0].reshape(NE, FC, P, D).transpose(0, 2, 1, 3)
    give("w_e", np.concatenate([gu.reshape(NE * P, -1), dn.reshape(NE * P, -1)], axis=1))

    outs = [("y_p", (1, SEQ, D)), ("y_s", (NB, NL, D)), ("mem_k", (1, 1, NM, XH, XD)), ("mem_v", (1, 1, NM, XH, XD)),
            ("chunk_v_p", (1, 1, P, HA, DHA)), ("chunk_v_s", (1, NB, NL, HA, DHA)), ("pool_p", (1, 1, HIST, WA)),
            ("pool_s", (1, NB, HIST, WA))]
    views = {"y_p": "a s d -> (a s) d", "y_s": "b l d -> (b l) d", "mem_k": "a b m h d -> (a b m) (h d)",
             "mem_v": "a b m h d -> (a b m) (h d)", "chunk_v_p": "a b t h d -> (a b t) (h d)",
             "chunk_v_s": "a b t h d -> (a b t) (h d)", "pool_p": "a b t c -> (a b t) c", "pool_s": "a b t c -> (a b) t c"}
    for n, s in outs:
        io[n] = nc.dram_tensor("out_" + n, s, F32, kind="ExternalOutput").ap().rearrange(views[n])
    build(nc, io)
    r = run_bass_kernel_spmd(nc, [arrays], core_ids=[0])
    return tuple(r.results[0]["out_" + n] for n, _ in outs)
```
